# Optimizing a Trainium2 kernel written in Bass

```python
import math
import jax, jax.numpy as jnp
from jax import lax
import numpy as np

D_MODEL = 1024
BATCH = 1
SEQ = 1024
DEPTH = 1

DA_HEADS = 4
DA_HEAD_DIM = 64
DA_V_DIM = 2 * DA_HEAD_DIM
DA_QK_WIDTH = DA_HEADS * 2 * DA_HEAD_DIM
DA_WIDTH = DA_HEADS * DA_V_DIM
Q_BLOCK = 128
HB_HEADS = 4
HB_HEAD_DIM = 64
HB_WIDTH = HB_HEADS * HB_HEAD_DIM
MAX_NEG_LOGIT = 80.0
GC_HEADS = 4
GC_KEY_DIM = 32
GC_VAL_DIM = 64
GC_KEY_WIDTH = GC_HEADS * GC_KEY_DIM
GC_WIDTH = GC_HEADS * GC_VAL_DIM
GC_GATE_RANK = 16
GC_GATE_NORMALIZER = 16.0
CHUNK = 64
N_BRANCH = 3
D_FF = 4 * D_MODEL
N_MOD = 6
EPS = 1e-6

IN_SIZES = (DA_QK_WIDTH, DA_QK_WIDTH, DA_WIDTH,
            HB_WIDTH, HB_WIDTH, HB_WIDTH, HB_WIDTH, HB_WIDTH,
            GC_KEY_WIDTH, GC_KEY_WIDTH, GC_WIDTH, GC_WIDTH,
            GC_GATE_RANK, GC_GATE_RANK,
            N_BRANCH * D_MODEL)
D_IN = (2 * DA_QK_WIDTH + DA_WIDTH + 5 * HB_WIDTH + 2 * GC_KEY_WIDTH + 2 * GC_WIDTH
        + 2 * GC_GATE_RANK + N_BRANCH * D_MODEL)


def rms_norm(x, g):
    xf = x.astype(jnp.float32)
    y = xf * lax.rsqrt(jnp.mean(xf * xf, axis=-1, keepdims=True) + EPS)
    return (y * g.astype(jnp.float32)).astype(x.dtype)

def split_cols(t, sizes):
    offs = np.cumsum(sizes)[:-1].tolist()
    return jnp.split(t, offs, axis=-1)

def to_heads(t, n_heads):
    b, s, w = t.shape
    return t.reshape(b, s, n_heads, w // n_heads).transpose(0, 2, 1, 3)

def from_heads(t):
    b, n, s, h = t.shape
    return t.transpose(0, 2, 1, 3).reshape(b, s, n * h)

def alibi_slopes(n):
    return jnp.array([2.0 ** (-8.0 * (i + 1) / n) for i in range(n)], dtype=jnp.float32)

def diff_attention(q, k, v, lam, slopes):
    b, h, _, s, d = q.shape
    nb = s // Q_BLOCK
    scale = d ** -0.5
    q_blocks = jnp.moveaxis(q.reshape(b, h, 2, nb, Q_BLOCK, d), 3, 0)
    starts = jnp.arange(nb, dtype=jnp.int32) * Q_BLOCK
    key_pos = jnp.arange(s, dtype=jnp.int32)

    def one_block(args):
        qb, start = args
        scores = jnp.einsum('bhiqd,bhikd->bhiqk', qb, k).astype(jnp.float32) * scale
        q_pos = start + jnp.arange(Q_BLOCK, dtype=jnp.int32)
        dist = jnp.abs(q_pos[:, None] - key_pos[None, :]).astype(jnp.float32)
        scores = scores - slopes[:, None, None, None] * dist
        p = jax.nn.softmax(scores, axis=-1)
        w = p[:, :, 0] - lam * p[:, :, 1]
        return jnp.einsum('bhqk,bhkv->bhqv', w.astype(v.dtype), v)

    out = lax.map(one_block, (q_blocks, starts))
    return jnp.moveaxis(out, 0, 2).reshape(b, h, s, v.shape[-1])

def chunk_scan(q, k, v, log_a):
    b, h, s, dk = q.shape
    dv = v.shape[-1]
    nc = s // CHUNK

    def to_chunks(t):
        return jnp.moveaxis(t.astype(jnp.float32).reshape(b, h, nc, CHUNK, t.shape[-1]), 2, 0)

    causal_in_chunk = jnp.tril(jnp.ones((CHUNK, CHUNK), dtype=bool))[:, :, None]

    def step(state, inp):
        qc, kc, vc, ac = inp
        cum = jnp.cumsum(ac, axis=2)
        o_inter = jnp.einsum('bhtk,bhkv->bhtv', qc * jnp.exp(cum), state)
        diff = cum[:, :, :, None, :] - cum[:, :, None, :, :]
        decay = jnp.where(causal_in_chunk, jnp.exp(jnp.where(causal_in_chunk, diff, 0.0)), 0.0)
        scores = jnp.einsum('bhtk,bhsk,bhtsk->bhts', qc, kc, decay)
        o_intra = jnp.einsum('bhts,bhsv->bhtv', scores, vc)
        last = cum[:, :, -1:, :]
        new_state = jnp.exp(last[:, :, 0, :])[..., None] * state + jnp.einsum(
            'bhsk,bhsv->bhkv', kc * jnp.exp(last - cum), vc)
        return new_state, o_inter + o_intra

    state0 = jnp.zeros((b, h, dk, dv), jnp.float32)
    _, o = lax.scan(step, state0, (to_chunks(q), to_chunks(k), to_chunks(v), to_chunks(log_a)))
    return jnp.moveaxis(o, 0, 2).reshape(b, h, s, dv)

def bidir_scan(q, k_fwd, k_bwd, v, la_fwd, la_bwd):
    flip = lambda t: jnp.flip(t, axis=2)
    fwd = chunk_scan(q, k_fwd, v, la_fwd)
    bwd = flip(chunk_scan(flip(q), flip(k_bwd), flip(v), flip(la_bwd)))
    return (fwd + bwd).astype(q.dtype)

def mixer_diff_attn(q_cols, k_cols, v_cols, lam_params, subln_g, layer_idx):
    b, s, _ = q_cols.shape

    def qk_heads(t):
        return t.reshape(b, s, DA_HEADS, 2, DA_HEAD_DIM).transpose(0, 2, 3, 1, 4)

    q = qk_heads(q_cols)
    k = qk_heads(k_cols)
    v = to_heads(v_cols, DA_HEADS)
    lam_init = 0.8 - 0.6 * math.exp(-0.3 * layer_idx)
    lp = lam_params.astype(jnp.float32)
    lam = jnp.exp(jnp.sum(lp[0] * lp[1])) - jnp.exp(jnp.sum(lp[2] * lp[3])) + lam_init
    o = diff_attention(q, k, v, lam, alibi_slopes(DA_HEADS))
    o = rms_norm(o, subln_g) * (1.0 - lam_init)
    return from_heads(o)

def mixer_hgrn2(q_cols, f_fwd_cols, f_bwd_cols, i_cols, g_cols, lower_bound, norm_g):
    q = jax.nn.silu(to_heads(q_cols, HB_HEADS)) * HB_HEAD_DIM ** -0.5
    v = to_heads(i_cols, HB_HEADS)

    def forget(cols, lb):
        z = to_heads(cols, HB_HEADS).astype(jnp.float32)
        lbh = lb.reshape(HB_HEADS, 1, HB_HEAD_DIM)
        log_f = jax.nn.log_sigmoid(z) + jnp.log1p(lbh * jnp.exp(jnp.minimum(-z, MAX_NEG_LOGIT)))
        k = (1.0 - lbh) * jax.nn.sigmoid(-z)
        return k, log_f

    k_f, la_f = forget(f_fwd_cols, lower_bound[0])
    k_b, la_b = forget(f_bwd_cols, lower_bound[1])
    o = rms_norm(bidir_scan(q, k_f, k_b, v, la_f, la_b), norm_g)
    return from_heads(o) * jax.nn.silu(g_cols)

def mixer_gla(q_cols, k_cols, v_cols, g_cols, lr_fwd, lr_bwd, gate_w2, gate_b, norm_g):
    q = to_heads(q_cols, GC_HEADS) * GC_KEY_DIM ** -0.5
    k = to_heads(k_cols, GC_HEADS)
    v = to_heads(v_cols, GC_HEADS)

    def log_decay(lr, w2, bias):
        z = (jnp.einsum('bsr,rk->bsk', lr, w2) + bias).astype(jnp.float32)
        return to_heads(jax.nn.log_sigmoid(z) / GC_GATE_NORMALIZER, GC_HEADS)

    la_f = log_decay(lr_fwd, gate_w2[0], gate_b[0])
    la_b = log_decay(lr_bwd, gate_w2[1], gate_b[1])
    o = rms_norm(bidir_scan(q, k, k, v, la_f, la_b), norm_g)
    return from_heads(o) * jax.nn.silu(g_cols)

def first_inputs(seed: int = 0) -> dict:
    key = jax.random.key(seed)
    ks = jax.random.split(key, 21)
    nrm = lambda k, shape, scale: jax.random.normal(k, shape, jnp.float32) * scale
    gain = lambda k, shape: 1.0 + 0.05 * jax.random.normal(k, shape, jnp.float32)
    return {
        "x": nrm(ks[0], (BATCH, SEQ, D_MODEL), 1.0),
        "c": nrm(ks[1], (BATCH, D_MODEL), 1.0),
        "ada_w": nrm(ks[2], (DEPTH, D_MODEL, N_MOD * D_MODEL), 0.5 * D_MODEL ** -0.5),
        "ada_b": nrm(ks[3], (DEPTH, N_MOD * D_MODEL), 0.02),
        "norm_mix_g": gain(ks[4], (DEPTH, D_MODEL)),
        "norm_mlp_g": gain(ks[5], (DEPTH, D_MODEL)),
        "w_in": nrm(ks[6], (DEPTH, D_MODEL, D_IN), D_MODEL ** -0.5),
        "diff_lambda": nrm(ks[7], (DEPTH, 4, DA_HEAD_DIM), 0.1),
        "diff_subln_g": gain(ks[8], (DEPTH, DA_V_DIM)),
        "hgrn_lb_logits": nrm(ks[9], (DEPTH, 2, HB_WIDTH), 0.1),
        "hgrn_norm_g": gain(ks[10], (DEPTH, HB_HEAD_DIM)),
        "gla_gate_w2": nrm(ks[11], (DEPTH, 2, GC_GATE_RANK, GC_KEY_WIDTH), GC_GATE_RANK ** -0.5),
        "gla_gate_b": nrm(ks[12], (DEPTH, 2, GC_KEY_WIDTH), 0.1),
        "gla_norm_g": gain(ks[13], (DEPTH, GC_VAL_DIM)),
        "w_up_a": nrm(ks[14], (DEPTH, DA_WIDTH, D_MODEL), DA_WIDTH ** -0.5),
        "w_up_b": nrm(ks[15], (DEPTH, HB_WIDTH, D_MODEL), HB_WIDTH ** -0.5),
        "w_up_c": nrm(ks[16], (DEPTH, GC_WIDTH, D_MODEL), GC_WIDTH ** -0.5),
        "w_out": nrm(ks[17], (DEPTH, D_MODEL, D_MODEL), D_MODEL ** -0.5),
        "mlp_w1": nrm(ks[18], (DEPTH, D_MODEL, D_FF), D_MODEL ** -0.5),
        "mlp_w2": nrm(ks[19], (DEPTH, D_FF, D_MODEL), D_FF ** -0.5),
        "final_norm_g": gain(ks[20], (D_MODEL,)),
    }

def first_block(x, c, ada_w, ada_b, norm_mix_g, norm_mlp_g, w_in, diff_lambda, diff_subln_g,
              hgrn_lb_logits, hgrn_norm_g, gla_gate_w2, gla_gate_b, gla_norm_g,
              w_up_a, w_up_b, w_up_c, w_out, mlp_w1, mlp_w2, final_norm_g):
    lb_w = jax.nn.softmax(hgrn_lb_logits.astype(jnp.float32), axis=0)
    lower_bounds = jnp.cumsum(lb_w, axis=0) - lb_w[0:1]
    cond = jax.nn.silu(c)
    for l in range(DEPTH):
        mod = cond @ ada_w[l] + ada_b[l]
        sh_m, sc_m, gt_m, sh_f, sc_f, gt_f = [t[:, None, :] for t in jnp.split(mod, N_MOD, axis=-1)]

        h = rms_norm(x, norm_mix_g[l]) * (1.0 + sc_m) + sh_m
        proj = jnp.einsum('bsd,de->bse', h, w_in[l])
        (a_q, a_k, a_v, b_q, b_ff, b_fb, b_i, b_g,
         c_q, c_k, c_v, c_g, c_lrf, c_lrb, gates) = split_cols(proj, IN_SIZES)
        o_a = mixer_diff_attn(a_q, a_k, a_v, diff_lambda[l], diff_subln_g[l], l)
        o_b = mixer_hgrn2(b_q, b_ff, b_fb, b_i, b_g, lower_bounds[l], hgrn_norm_g[l])
        o_c = mixer_gla(c_q, c_k, c_v, c_g, c_lrf, c_lrb, gla_gate_w2[l], gla_gate_b[l], gla_norm_g[l])
        g_a, g_b, g_c = jnp.split(jax.nn.sigmoid(gates), N_BRANCH, axis=-1)
        merged = g_a * (o_a @ w_up_a[l]) + g_b * (o_b @ w_up_b[l]) + g_c * (o_c @ w_up_c[l])
        x = x + gt_m * (merged @ w_out[l])

        h = rms_norm(x, norm_mlp_g[l]) * (1.0 + sc_f) + sh_f
        x = x + gt_f * (jnp.square(jax.nn.relu(h @ mlp_w1[l])) @ mlp_w2[l])
    return rms_norm(x, final_norm_g)


DEPTH_2 = 2

HEAD_DIM = 64
ROPE_THETA = 500000.0
ROT_DIM = HEAD_DIM // 4
GRID_W = 64
NEG_INF = -1e30
QBLK = 128

A_HEADS = 3 * D_MODEL // (4 * HEAD_DIM)
A_WIDTH = A_HEADS * HEAD_DIM
A_PATTERNS = ((128, 1), (512, 4), (2048, 16))
B_GROUP_DIM = 64
B_GROUPS = D_MODEL // (4 * B_GROUP_DIM)
B_WIDTH = B_GROUPS * B_GROUP_DIM
B_CHUNK = 128
EVEN_IN = 3 * A_WIDTH + 2 * B_WIDTH
C_HEADS = D_MODEL // (2 * HEAD_DIM)
C_Q_RANK = D_MODEL // 4
C_KV_RANK = D_MODEL // 8
C_NOPE = HEAD_DIM
C_ROPE = HEAD_DIM // 2
C_V = HEAD_DIM
D_HEADS = D_MODEL // (2 * HEAD_DIM)
D_KV_HEADS = 2
D_GROUP = D_HEADS // D_KV_HEADS
D_THETA = 10000.0
ODD_IN = C_Q_RANK + C_KV_RANK + C_ROPE + (D_HEADS + 2 * D_KV_HEADS) * HEAD_DIM
N_EXPERTS = 16
EC_FACTOR = 2
EXPERT_FF = 512


def rmsnorm(x, g):
    xf = x.astype(jnp.float32)
    y = xf * lax.rsqrt(jnp.mean(xf * xf, axis=-1, keepdims=True) + EPS)
    return (y * g.astype(jnp.float32)).astype(x.dtype)

def rope(x, pos, theta):
    r = x.shape[-1]
    half = r // 2
    inv = jnp.power(jnp.float32(theta), -jnp.arange(half, dtype=jnp.float32) * (2.0 / r))
    ang = pos.astype(jnp.float32)[:, None] * inv[None, :]
    shape = (pos.shape[0],) + (1,) * (x.ndim - 3) + (half,)
    cos = jnp.cos(ang).reshape(shape)
    sin = jnp.sin(ang).reshape(shape)
    xf = x.astype(jnp.float32)
    x1, x2 = xf[..., :half], xf[..., half:]
    return jnp.concatenate([x1 * cos - x2 * sin, x1 * sin + x2 * cos], axis=-1).astype(x.dtype)

def partial_rope(x, pos):
    return jnp.concatenate([rope(x[..., :ROT_DIM], pos, ROPE_THETA), x[..., ROT_DIM:]], axis=-1)

def axial_rope(x, row, col):
    half = x.shape[-1] // 2
    return jnp.concatenate([rope(x[..., :half], row, D_THETA), rope(x[..., half:], col, D_THETA)], axis=-1)

def dilated_band_attention(q, k, v, window, dilation):
    b, s, h, dh = q.shape
    r = window // (2 * dilation)
    blk = r
    L = s // dilation
    nb = -(-L // blk)
    lp = nb * blk

    def residue(t):
        return t.reshape(b, L, dilation, h, dh).transpose(0, 2, 1, 3, 4)

    qr = jnp.pad(residue(q), ((0, 0), (0, 0), (0, lp - L), (0, 0), (0, 0)))
    qr = qr.reshape(b, dilation, nb, blk, h, dh)

    def band(t):
        tp = jnp.pad(residue(t), ((0, 0), (0, 0), (blk, lp - L + blk), (0, 0), (0, 0)))
        tp = tp.reshape(b, dilation, nb + 2, blk, h, dh)
        return jnp.concatenate([tp[:, :, 0:nb], tp[:, :, 1:nb + 1], tp[:, :, 2:nb + 2]], axis=3)

    kb, vb = band(k), band(v)
    scores = jnp.einsum('bdnqhc,bdnkhc->bdnhqk', qr, kb).astype(jnp.float32) * (dh ** -0.5)
    qi = jnp.arange(blk)[:, None]
    ki = jnp.arange(3 * blk)[None, :]
    in_band = jnp.abs(ki - blk - qi) <= r
    kpos = jnp.arange(nb)[:, None] * blk - blk + jnp.arange(3 * blk)[None, :]
    valid = in_band[None] & ((kpos >= 0) & (kpos < L))[:, None, :]
    scores = jnp.where(valid[None, None, :, None], scores, NEG_INF)
    lse = jax.nn.logsumexp(scores, axis=-1)
    p = jnp.exp(scores - lse[..., None])
    out = jnp.einsum('bdnhqk,bdnkhc->bdnqhc', p.astype(v.dtype), vb)
    out = out.reshape(b, dilation, lp, h, dh)[:, :, :L].transpose(0, 2, 1, 3, 4).reshape(b, s, h, dh)
    lse = lse.transpose(0, 1, 2, 4, 3).reshape(b, dilation, lp, h)[:, :, :L]
    lse = lse.transpose(0, 2, 1, 3).reshape(b, s, h)
    return out, lse

def dilated_mixture(q, k, v):
    results = [dilated_band_attention(q, k, v, w, d) for (w, d) in A_PATTERNS]
    outs = jnp.stack([o for (o, _) in results], axis=0)
    lses = jnp.stack([l for (_, l) in results], axis=0)
    wts = jax.nn.softmax(lses, axis=0)
    return jnp.einsum('pbsh,pbshc->bshc', wts.astype(q.dtype), outs)

def spatial_gating(z, v_norm, w_s, b_s):
    b, s, _ = z.shape
    z = jax.nn.gelu(z)
    u, vv = jnp.split(z, 2, axis=-1)
    u = u.reshape(b, s, B_GROUPS, B_GROUP_DIM)
    vv = rmsnorm(vv.reshape(b, s, B_GROUPS, B_GROUP_DIM), v_norm)
    vv = vv.reshape(b, s // B_CHUNK, B_CHUNK, B_GROUPS, B_GROUP_DIM)
    mixed = jnp.einsum('gpq,bnqgc->bnpgc', w_s, vv) + b_s.T[None, None, :, :, None]
    return (u * mixed.reshape(b, s, B_GROUPS, B_GROUP_DIM)).reshape(b, s, B_WIDTH)

def block_attention(q, k, v):
    b, s, kvh, g, dk = q.shape
    nq = s // QBLK
    scale = dk ** -0.5
    qb = q.reshape(b, nq, QBLK, kvh, g, dk).transpose(1, 0, 2, 3, 4, 5)

    def one(qblk):
        sc = jnp.einsum('bqkgc,bskc->bkgqs', qblk, k).astype(jnp.float32) * scale
        p = jax.nn.softmax(sc, axis=-1)
        return jnp.einsum('bkgqs,bskc->bqkgc', p.astype(v.dtype), v)

    out = lax.map(one, qb)
    return out.transpose(1, 0, 2, 3, 4, 5).reshape(b, s, kvh * g * v.shape[-1])

def mixer_even(h, pos, w_in, gmlp_norm, w_s, b_s, w_out):
    b, s, _ = h.shape
    proj = h @ w_in
    q, k, v, z = jnp.split(proj, [A_WIDTH, 2 * A_WIDTH, 3 * A_WIDTH], axis=-1)
    q = partial_rope(q.reshape(b, s, A_HEADS, HEAD_DIM), pos)
    k = partial_rope(k.reshape(b, s, A_HEADS, HEAD_DIM), pos)
    v = v.reshape(b, s, A_HEADS, HEAD_DIM)
    a_out = dilated_mixture(q, k, v).reshape(b, s, A_WIDTH)
    g_out = spatial_gating(z, gmlp_norm, w_s, b_s)
    return jnp.concatenate([a_out, g_out], axis=-1) @ w_out

def mixer_odd(h, pos, row, col, w_in, cq_norm, w_cq_up, ckv_norm, w_ckv_up, dq_norm, dk_norm, w_out):
    b, s, _ = h.shape
    proj = h @ w_in
    o1 = C_Q_RANK
    o2 = o1 + C_KV_RANK
    o3 = o2 + C_ROPE
    o4 = o3 + D_HEADS * HEAD_DIM
    o5 = o4 + D_KV_HEADS * HEAD_DIM
    cq, ckv, ck_rope, dq, dk, dv = jnp.split(proj, [o1, o2, o3, o4, o5], axis=-1)
    cq = (rmsnorm(cq, cq_norm) @ w_cq_up).reshape(b, s, C_HEADS, C_NOPE + C_ROPE)
    q_nope, q_rope = cq[..., :C_NOPE], rope(cq[..., C_NOPE:], pos, ROPE_THETA)
    kv = (rmsnorm(ckv, ckv_norm) @ w_ckv_up).reshape(b, s, C_HEADS, C_NOPE + C_V)
    k_nope, v_c = kv[..., :C_NOPE], kv[..., C_NOPE:]
    k_rope = rope(ck_rope, pos, ROPE_THETA)
    q_c = jnp.concatenate([q_nope, q_rope], axis=-1)[:, :, :, None]
    k_c = jnp.concatenate([k_nope, jnp.broadcast_to(k_rope[:, :, None], (b, s, C_HEADS, C_ROPE))], axis=-1)
    c_out = block_attention(q_c, k_c, v_c)
    dq = axial_rope(rmsnorm(dq.reshape(b, s, D_KV_HEADS, D_GROUP, HEAD_DIM), dq_norm), row, col)
    dk = axial_rope(rmsnorm(dk.reshape(b, s, D_KV_HEADS, HEAD_DIM), dk_norm), row, col)
    dv = dv.reshape(b, s, D_KV_HEADS, HEAD_DIM)
    d_out = block_attention(dq, dk, dv)
    return jnp.concatenate([c_out, d_out], axis=-1) @ w_out

def ec_moe(h, w_router, w_gate, w_up, w_down):
    b, s, d = h.shape
    cap = EC_FACTOR * s // N_EXPERTS
    logits = jnp.einsum('bsd,de->bse', h, w_router).astype(jnp.float32)
    aff = jax.nn.softmax(logits, axis=-1)
    gates, idx = lax.top_k(aff.transpose(0, 2, 1), cap)
    xs = jax.vmap(lambda hb, ib: hb[ib])(h, idx)
    g = jnp.einsum('becd,edf->becf', xs, w_gate)
    u = jnp.einsum('becd,edf->becf', xs, w_up)
    y = jnp.einsum('becf,efd->becd', jax.nn.silu(g) * u, w_down)
    y = y * gates[..., None].astype(y.dtype)
    return jax.vmap(lambda ib, yb: jnp.zeros((s, d), yb.dtype).at[ib.reshape(-1)].add(yb.reshape(-1, d)))(idx, y)

def second_inputs(seed: int = 0) -> dict:
    key = jax.random.key(seed)
    ks = jax.random.split(key, 21)
    n_even = (DEPTH_2 + 1) // 2
    n_odd = DEPTH_2 // 2

    def normal(k, shape, scale):
        return jax.random.normal(k, shape, jnp.float32) * scale

    def gain(k, shape):
        return 1.0 + 0.02 * jax.random.normal(k, shape, jnp.float32)

    return {
        "x": normal(ks[0], (BATCH, SEQ, D_MODEL), 1.0),
        "norm_mix": gain(ks[1], (DEPTH_2, D_MODEL)),
        "norm_ffn": gain(ks[2], (DEPTH_2, D_MODEL)),
        "even_w_in": normal(ks[3], (n_even, D_MODEL, EVEN_IN), D_MODEL ** -0.5),
        "even_gmlp_norm": gain(ks[4], (n_even, B_GROUPS, B_GROUP_DIM)),
        "even_w_spatial": normal(ks[5], (n_even, B_GROUPS, B_CHUNK, B_CHUNK), B_CHUNK ** -0.5),
        "even_b_spatial": normal(ks[6], (n_even, B_GROUPS, B_CHUNK), 0.02),
        "even_w_out": normal(ks[7], (n_even, A_WIDTH + B_WIDTH, D_MODEL), (A_WIDTH + B_WIDTH) ** -0.5),
        "odd_w_in": normal(ks[8], (n_odd, D_MODEL, ODD_IN), D_MODEL ** -0.5),
        "odd_cq_norm": gain(ks[9], (n_odd, C_Q_RANK)),
        "odd_w_cq_up": normal(ks[10], (n_odd, C_Q_RANK, C_HEADS * (C_NOPE + C_ROPE)), C_Q_RANK ** -0.5),
        "odd_ckv_norm": gain(ks[11], (n_odd, C_KV_RANK)),
        "odd_w_ckv_up": normal(ks[12], (n_odd, C_KV_RANK, C_HEADS * (C_NOPE + C_V)), C_KV_RANK ** -0.5),
        "odd_dq_norm": gain(ks[13], (n_odd, HEAD_DIM)),
        "odd_dk_norm": gain(ks[14], (n_odd, HEAD_DIM)),
        "odd_w_out": normal(ks[15], (n_odd, C_HEADS * C_V + D_HEADS * HEAD_DIM, D_MODEL), (C_HEADS * C_V + D_HEADS * HEAD_DIM) ** -0.5),
        "moe_w_router": normal(ks[16], (DEPTH_2, D_MODEL, N_EXPERTS), D_MODEL ** -0.5),
        "moe_w_gate": normal(ks[17], (DEPTH_2, N_EXPERTS, D_MODEL, EXPERT_FF), D_MODEL ** -0.5),
        "moe_w_up": normal(ks[18], (DEPTH_2, N_EXPERTS, D_MODEL, EXPERT_FF), D_MODEL ** -0.5),
        "moe_w_down": normal(ks[19], (DEPTH_2, N_EXPERTS, EXPERT_FF, D_MODEL), EXPERT_FF ** -0.5),
        "final_norm": gain(ks[20], (D_MODEL,)),
    }

def second_block(x, norm_mix, norm_ffn, even_w_in, even_gmlp_norm, even_w_spatial, even_b_spatial, even_w_out,
              odd_w_in, odd_cq_norm, odd_w_cq_up, odd_ckv_norm, odd_w_ckv_up, odd_dq_norm, odd_dk_norm, odd_w_out,
              moe_w_router, moe_w_gate, moe_w_up, moe_w_down, final_norm):
    b, s, _ = x.shape
    pos = jnp.arange(s, dtype=jnp.int32)
    rows = s // GRID_W
    row = jnp.repeat(jnp.arange(rows, dtype=jnp.int32), GRID_W)
    col = jnp.tile(jnp.arange(GRID_W, dtype=jnp.int32), rows)
    for i in range(DEPTH_2):
        j = i // 2
        h = rmsnorm(x, norm_mix[i])
        if i % 2 == 0:
            mix = mixer_even(h, pos, even_w_in[j], even_gmlp_norm[j], even_w_spatial[j], even_b_spatial[j], even_w_out[j])
        else:
            mix = mixer_odd(h, pos, row, col, odd_w_in[j], odd_cq_norm[j], odd_w_cq_up[j], odd_ckv_norm[j],
                            odd_w_ckv_up[j], odd_dq_norm[j], odd_dk_norm[j], odd_w_out[j])
        x = x + mix
        x = x + ec_moe(rmsnorm(x, norm_ffn[i]), moe_w_router[i], moe_w_gate[i], moe_w_up[i], moe_w_down[i])
    return rmsnorm(x, final_norm)


def setup_inputs(seed=0):
    out = dict(first_inputs(seed))
    for name, value in second_inputs(seed + 1).items():
        if name != "x":
            out[name + "_2"] = value
    return out


def reference(
    x, c, ada_w, ada_b, norm_mix_g, norm_mlp_g, w_in, diff_lambda, diff_subln_g, hgrn_lb_logits,
    hgrn_norm_g, gla_gate_w2, gla_gate_b, gla_norm_g, w_up_a, w_up_b, w_up_c, w_out, mlp_w1,
    mlp_w2, final_norm_g, norm_mix_2, norm_ffn_2, even_w_in_2, even_gmlp_norm_2,
    even_w_spatial_2, even_b_spatial_2, even_w_out_2, odd_w_in_2, odd_cq_norm_2, odd_w_cq_up_2,
    odd_ckv_norm_2, odd_w_ckv_up_2, odd_dq_norm_2, odd_dk_norm_2, odd_w_out_2, moe_w_router_2,
    moe_w_gate_2, moe_w_up_2, moe_w_down_2, final_norm_2,
):
    x = first_block(
        x, c, ada_w, ada_b, norm_mix_g, norm_mlp_g, w_in, diff_lambda, diff_subln_g,
        hgrn_lb_logits, hgrn_norm_g, gla_gate_w2, gla_gate_b, gla_norm_g, w_up_a, w_up_b,
        w_up_c, w_out, mlp_w1, mlp_w2, final_norm_g,
    )
    return second_block(
        x, norm_mix_2, norm_ffn_2, even_w_in_2, even_gmlp_norm_2, even_w_spatial_2,
        even_b_spatial_2, even_w_out_2, odd_w_in_2, odd_cq_norm_2, odd_w_cq_up_2,
        odd_ckv_norm_2, odd_w_ckv_up_2, odd_dq_norm_2, odd_dk_norm_2, odd_w_out_2,
        moe_w_router_2, moe_w_gate_2, moe_w_up_2, moe_w_down_2, final_norm_2,
    )


_drawn_inputs = setup_inputs


def setup_inputs(seed=0):
    import zlib

    import numpy as np

    out = dict(_drawn_inputs(seed))
    spreads = {}
    factors = {'diff_subln_g': 4.325,
     'hgrn_norm_g': 4.165,
     'gla_gate_b': 4.848,
     'gla_norm_g': 4.706,
     'norm_mix_2': 2.85,
     'even_gmlp_norm_2': 4.384,
     'even_b_spatial_2': 4.292,
     'odd_cq_norm_2': 8.0,
     'odd_ckv_norm_2': 8.0,
     'odd_dq_norm_2': 8.0,
     'odd_dk_norm_2': 8.0,
     'final_norm_2': 2.837}
    for name, (base, spread) in spreads.items():
        noise = np.random.default_rng([zlib.crc32(name.encode()), seed]).standard_normal(out[name].shape)
        drawn = base * np.exp(spread * noise) if base else spread * noise
        out[name] = __import__('jax').numpy.asarray(drawn.astype(out[name].dtype))
    for name, factor in factors.items():
        out[name] = (out[name] * factor).astype(out[name].dtype)
    return out
```

```python
import concourse.bass as bass
from concourse import mybir
from concourse.alu_op_type import AluOpType as ALU
from contextlib import ExitStack
import numpy as np

F32 = mybir.dt.float32
F32R = mybir.dt.float32r
U32 = mybir.dt.uint32
U8 = mybir.dt.uint8
ACT = mybir.ActivationFunctionType
AX = mybir.AxisListType

P = 128
S = 1024
D = 1024
NT = S // P
KD = D // P
HALF = 512
EPS = 1e-6
SLOT = KD * HALF
RING = 4
LOWEST = -3.0e38


class Stage:

    def __init__(self, nc, name):
        self.nc, self.name, self.ctx, self.sems = nc, name, ExitStack(), []

    def __enter__(self):
        return self

    def __exit__(self, *exc):
        self.ctx.__exit__(*exc)
        self.nc.clear_and_free_semaphores(self.sems)
        self.nc.all_engine_barrier()

    def sb(self, name, shape, dt=F32):
        return self.ctx.enter_context(self.nc.sbuf_tensor(f"{self.name}_{name}", shape, dt))

    def ps(self, name, shape):
        return self.ctx.enter_context(self.nc.psum_tensor(f"{self.name}_{name}", shape, F32))

    def sem(self, name):
        self.sems.append(self.nc.alloc_semaphore(f"{self.name}_{name}"))
        return self.sems[-1]

    def block(self):
        return self.ctx.enter_context(self.nc.Block())


class Steps:

    def __init__(self, eng, sem):
        self.eng, self.sem, self.n, self.base = eng, sem, 0, 0

    def __call__(self, ins):
        ins.then_inc(self.sem, 1)
        self.n += 1
        self.eng.wait_ge(self.sem, self.base + self.n)

    def turn(self, i, per):
        self.start, self.per, self.base = self.n, per, i * per

    def turned(self, turns):
        assert self.n - self.start == self.per, (self.n - self.start, self.per)
        self.n, self.base = self.start + self.per * turns, 0


class Ring:

    def __init__(self, nc, ctx, w_all):
        self.w, self.total = w_all, w_all.shape[0]
        self.buf, self.buf_r = twin_buffer(nc, ctx, "ring", [P, RING, SLOT])
        self.ready = [ctx.enter_context(nc.semaphore(f"slot_ready{j}")) for j in range(RING)]
        self.free = ctx.enter_context(nc.semaphore("slots_free"))
        self.issued = self.used = 0
        self.limit = self.total

    def take(self, count):
        first, self.used = self.used, self.used + count
        return first

    def slot(self, g, k, n):
        return self.buf[:, g % RING, 0:k * n].rearrange("p (k n) -> p k n", k=k)

    def wait(self, eng, g, i=0, per=0):
        assert per % RING == 0
        eng.wait_ge(self.ready[g % RING], i * (per // RING * 16) + 16 * (g // RING + 1))

    def release(self, eng):
        eng.nop().then_inc(self.free, 1)

    def feed(self, sp):
        upto = min(self.used + RING, self.limit)

        def load(g, row, freed):
            if freed is not None:
                sp.wait_ge(self.free, freed)
            sp.dma_start(self.buf[:, g % RING, :], self.w[row, :, :]).then_inc(self.ready[g % RING], 16)

        while self.issued < upto:
            g = self.issued
            turns = (upto - g) // RING
            if g % RING == 0 and g >= RING and turns > 1:
                with sp.Fori(0, turns) as i:
                    for j in range(RING):
                        sp.wait_ge(self.free, i * RING + (g + j - RING + 1))
                        sp.dma_start(self.buf[:, j, :], self.w[bass.ds(i * RING + (g + j), 1), :, :]
                                     .rearrange("o p n -> (o p) n")).then_inc(self.ready[j], 16)
                self.issued += turns * RING
            else:
                load(g, g, g - RING + 1 if g >= RING else None)
                self.issued += 1


def twin_buffer(nc, ctx, name, shape):
    with nc.sbuf_tensor(f"{name}_r", shape, F32R) as reduced:
        pass
    return ctx.enter_context(nc.sbuf_tensor(name, shape, F32)), reduced


def split(step, dve, x, high, low):
    step(dve.tensor_copy(high, x))
    return dve.tensor_tensor(low, x, high.bitcast(F32), ALU.subtract)


def three_passes(pe, out, left, right, start, stop):
    (lh, ll), (rh, rl) = left, right
    pe.matmul(out, lh, rh, start=start, stop=False)
    pe.matmul(out, lh, rl, start=False, stop=False)
    return pe.matmul(out, ll, rh, start=False, stop=stop)


def mod_stage(nc, m):
    with Stage(nc, "mod") as st:
        NCH = 6 * D // HALF
        first = m["ring"].take(NCH)
        ccol, cact = st.sb("ccol", [P, KD]), st.sb("cact", [P, KD])
        cwide = st.sb("cwide", [P, KD, P])
        bias, mod = st.sb("bias", [P, NCH, HALF]), st.sb("mod", [P, NCH, HALF])
        out = st.ps("out", [P, 2, HALF])
        loaded, act_done, wide, summed, added, stored = (
            st.sem(x) for x in ("loaded", "act_done", "wide", "summed", "added", "stored"))
        block = st.block()

        @block.sync
        def _(sp):
            m["ring"].feed(sp)

        @block.gpsimd
        def _(pool):
            pool.dma_start(ccol[:], m["c_col"]).then_inc(loaded, 16)
            pool.dma_start(m["ident"][:], m["ident_dram"]).then_inc(m["ident_in"], 16)
            pool.dma_start(bias[:], m["ada_b"].rearrange("p (c n) -> p c n", n=HALF)).then_inc(loaded, 16)
            pool.wait_ge(added, 2 + NCH)
            pool.dma_start(m["mod"].rearrange("p (c n) -> p c n", n=HALF), mod[:]).then_inc(stored, 16)
            pool.wait_ge(stored, 16)

        @block.scalar
        def _(act):
            act.wait_ge(loaded, 32)
            act.activation(cact[:], ccol[:], ACT.Silu).then_inc(act_done, 1)

        @block.vector
        def _(dve):
            dve.nop().then_inc(added, 2)
            dve.wait_ge(act_done, 1)
            dve.tensor_copy(cwide[:], cact[:, :].unsqueeze(2).to_broadcast([P, KD, P])).then_inc(wide, 1)
            with dve.Fori(0, NCH // 4) as i:
                for j in range(4):
                    dve.wait_ge(summed, i * 4 + (j + 1))
                    m["ring"].release(dve)
                    dve.tensor_tensor(mod[:, bass.ds(i * 4 + j, 1), :].rearrange("p o n -> p (o n)"), out[:, j % 2, :],
                                      bias[:, bass.ds(i * 4 + j, 1), :].rearrange("p o n -> p (o n)"),
                                      ALU.add).then_inc(added, 1)

        @block.tensor
        def _(pe):
            pe.wait_ge(wide, 1)
            with pe.Fori(0, NCH // 4) as i:
                for j in range(4):
                    w = m["ring"].slot(first + j, KD, HALF)
                    m["ring"].wait(pe, first + j, i, 4)
                    pe.wait_ge(added, i * 4 + (j + 1))
                    for k in range(KD):
                        ins = pe.matmul(out[:, j % 2, :], cwide[:, k, :], w[:, k, :], start=k == 0, stop=k == KD - 1)
                    ins.then_inc(summed, 1)


def norm_stage(nc, m, name, src, gain, scale=None, shift=None, keep=None, turned=True, ahead=None):
    with Stage(nc, name) as st:
        x = st.sb("x", [P, NT, D])
        h = st.sb("h", [P, 2, D])
        g, sc, sh = st.sb("gain", [P, D]), st.sb("scale", [P, D]), st.sb("shift", [P, D])
        junk = h[:, 0, :]
        ss, rs = st.sb("ss", [P, NT]), st.sb("rs", [P, NT])
        tp = st.ps("tp", [P, 2, KD, P])
        x_in = [st.sem(f"x_in{t}") for t in range(NT)]
        par_in, squared, mean_in, root, dve_done, h_ready, h_free, turned_up, tp_free, stored, kept, stepped = (
            st.sem(x_) for x_ in ("par_in", "squared", "mean_in", "root", "dve_done", "h_ready", "h_free",
                                  "turned_up", "tp_free", "stored", "kept", "stepped"))
        block = st.block()
        readers = [x_ for x_, used in ((h_free, turned), (kept, keep is not None)) if used]
        mod = scale is not None

        @block.sync
        def _(sp):
            for t in range(NT):
                sp.dma_start(x[:, t, :], src[t * P:(t + 1) * P, :]).then_inc(x_in[t], 16)
            sp.dma_start(g[:], gain).then_inc(par_in, 16)
            if mod:
                sp.dma_start(sc[:], m["mod"][:, scale * D:(scale + 1) * D]).then_inc(par_in, 16)
                sp.dma_start(sh[:], m["mod"][:, shift * D:(shift + 1) * D]).then_inc(par_in, 16)
            m["ring"].feed(sp)
            if ahead is not None:
                ahead(sp)

        @block.scalar
        def _(act):
            for t in range(NT):
                act.wait_ge(x_in[t], 16)
                act.activation(junk, x[:, t, :], ACT.Square, accum_out=ss[:, t:t + 1]).then_inc(squared, 1)
                act.wait_ge(squared, t + 1)
            act.wait_ge(mean_in, 1)
            act.activation(rs[:], ss[:], ACT.Sqrt).then_inc(root, 1)
            if turned:
                act.nop().then_inc(tp_free, 2)
                act.nop().then_inc(h_free, 2)
                with act.Fori(0, NT // 2) as i:
                    for b in range(2):
                        act.wait_ge(turned_up, i * 2 + (b + 1))
                        act.nop().then_inc(h_free, 1)
                        act.activation(m["hT"][:, :, bass.ds(i * 2 * P + b * P, P)], tp[:, b, :, :],
                                       ACT.Copy).then_inc(tp_free, 1)

        @block.vector
        def _(dve):
            step = Steps(dve, stepped)
            dve.wait_ge(par_in, 48 if mod else 16)
            if mod:
                step(dve.scalar_tensor_tensor(g[:], sc[:], 1.0, g[:], ALU.add, ALU.mult))
            dve.wait_ge(squared, NT)
            dve.tensor_scalar(ss[:], ss[:], 1.0 / D, EPS, ALU.mult, ALU.add).then_inc(mean_in, 1)
            dve.wait_ge(root, 1)
            step(dve.reciprocal(rs[:], rs[:]))
            with dve.Fori(0, NT // 2) as i:
                for b in range(2):
                    for reader in readers:
                        dve.wait_ge(reader, i * 2 + (b + 1))
                    xt = x[:, bass.ds(i * 2 + b, 1), :].rearrange("p o n -> p (o n)")
                    ins = dve.scalar_tensor_tensor(h[:, b, :], xt, rs[:, bass.ds(i * 2 + b, 1)], g[:],
                                                   ALU.mult, ALU.mult)
                    if mod:
                        ins.then_inc(dve_done, 1)
                        dve.wait_ge(dve_done, i * 2 + (b + 1))
                        ins = dve.tensor_tensor(h[:, b, :], h[:, b, :], sh[:], ALU.add)
                    ins.then_inc(h_ready, 1)

        @block.gpsimd
        def _(pool):
            if keep is not None:
                pool.nop().then_inc(kept, 2)
                with pool.Fori(0, NT // 2) as i:
                    for b in range(2):
                        pool.wait_ge(h_ready, i * 2 + (b + 1))
                        pool.dma_start(keep[bass.ds(i * 2 * P + b * P, P), :], h[:, b, :]).then_inc(stored, 16)
                        pool.wait_ge(stored, i * 32 + 16 * (b + 1))
                        pool.nop().then_inc(kept, 1)

        if turned:
            @block.tensor
            def _(pe):
                pe.wait_ge(m["ident_in"], 16)
                with pe.Fori(0, NT // 2) as i:
                    for b in range(2):
                        pe.wait_ge(h_ready, i * 2 + (b + 1))
                        pe.wait_ge(tp_free, i * 2 + (b + 1))
                        for k in range(KD):
                            ins = pe.transpose(tp[:, b, k, :], h[:, b, k * P:(k + 1) * P], m["ident"][:])
                        ins.then_inc(turned_up, 1)


def per_turn(eng, turns, body):
    with eng.Fori(0, turns - 1) as i:
        body(i, True)
    body(turns - 1, False)


def start(eng, *sems):
    for s in sems:
        eng.nop().then_inc(s, 2)


def group_squares(step, dve, x, tmp, ss):
    step(dve.tensor_tensor(tmp, x, x, ALU.mult))
    step(dve.tensor_reduce(ss, tmp, AX.X, ALU.add))


def rope(step, dve, x1, x2, cos, sin, tmp):
    a, b, c, d = tmp
    dve.tensor_tensor(a, x1, cos, ALU.mult)
    dve.tensor_tensor(b, x2, sin, ALU.mult)
    dve.tensor_tensor(c, x1, sin, ALU.mult)
    step(dve.tensor_tensor(d, x2, cos, ALU.mult))
    dve.tensor_tensor(x1, a, b, ALU.subtract)
    step(dve.tensor_tensor(x2, c, d, ALU.add))


class Attention:

    def __init__(self, st, units, maps, scale, bias=None):
        self.units, self.maps, self.scale, self.bias = units, maps, scale, bias
        self.n_sc = 2 * maps
        self.S = st.ps("scores", [P, 4, HALF])
        self.TP = st.ps("turned", [P, NT, P])
        self.O = st.ps("outs", [P, 2, HALF])
        self.sc = st.sb("sc", [P, self.n_sc, S])
        self.pT = st.sb("pT", [P, 2, NT, P])
        self.nm = st.sb("nm", [P, self.n_sc])
        self.wait_taker = st.sb("wait_taker", [P, 1])
        self.rs = st.sb("rs", [P, 4 * maps])
        self.ri = st.sb("ri", [P, 4 * maps])
        (self.scored, self.s_free, self.shifted, self.exped, self.mixed, self.turned_p, self.tp_free,
         self.sc_free, self.evacuated, self.pv_done, self.out_done) = (
            st.sem(x) for x in ("scored", "s_free", "shifted", "exped", "mixed", "turned_p", "tp_free",
                                "sc_free", "evacuated", "pv_done", "out_done"))

    def score_view(self, n):
        b = 2 * (n % 2)
        return self.S[:, b:b + 2, :].rearrange("p a n -> p (a n)")

    def begin_act(self, act):
        start(act, self.sc_free)
        act.nop().then_inc(self.tp_free, 1)
        if self.bias is None:
            start(act, self.s_free)

    def begin_dve(self, dve):
        start(dve, self.out_done)
        if self.bias is not None:
            start(dve, self.s_free)

    def pe(self, pe, i, queries, keys, values, ident):
        U, M = self.units, self.maps
        for u in range(-1, U + 1):
            if u + 1 < U:
                for mp in range(M):
                    n = (u + 1) * M + mp
                    pe.wait_ge(self.s_free, i * (U * M) + (n + 1))
                    q, k = queries(u + 1, mp), keys(u + 1, mp)
                    b = 2 * (n % 2)
                    pe.matmul(self.S[:, b, :], q, k[:, 0:HALF], start=True, stop=True)
                    pe.matmul(self.S[:, b + 1, :], q, k[:, HALF:S], start=True, stop=True).then_inc(self.scored, 1)
            if 0 <= u < U:
                pe.wait_ge(self.mixed if M == 2 else self.exped, i * U + (u + 1))
                pe.wait_ge(self.tp_free, i * U + (u + 1))
                p = self.sc[:, (u * M) % self.n_sc, :]
                for kb in range(NT):
                    ins = pe.transpose(self.TP[:, kb, :], p[:, kb * P:(kb + 1) * P], ident)
                ins.then_inc(self.turned_p, 1)
            if u >= 1:
                w = u - 1
                v = values(w)
                pe.wait_ge(self.evacuated, i * U + (w + 1))
                pe.wait_ge(self.out_done, i * U + (w + 1))
                for kb in range(NT):
                    ins = pe.matmul(self.O[:, w % 2, 0:v.shape[2]], self.pT[:, w % 2, kb, :], v[:, kb, :],
                                    start=kb == 0, stop=kb == NT - 1)
                ins.then_inc(self.pv_done, 1)

    def act(self, act, i):
        U, M = self.units, self.maps
        for u in range(-1, U):
            if u + 1 < U:
                for mp in range(M):
                    n = (u + 1) * M + mp
                    act.wait_ge(self.shifted, i * (U * M) + (n + 1))
                    sc = self.sc[:, n % self.n_sc, :]
                    nm, rs = self.nm[:, n % self.n_sc:n % self.n_sc + 1], n % (4 * M)
                    if self.bias is not None:
                        act.activation(sc, sc, ACT.Exp, bias=nm, scale=-1.0,
                                       accum_out=self.rs[:, rs:rs + 1]).then_inc(self.exped, 1)
                    else:
                        act.activation(sc, self.score_view(n), ACT.Exp, bias=nm, scale=self.scale,
                                       accum_out=self.rs[:, rs:rs + 1]).then_inc(self.exped, 1)
                        act.wait_ge(self.exped, i * (U * M) + (n + 1))
                        act.nop().then_inc(self.s_free, 1)
            if u >= 0:
                act.wait_ge(self.turned_p, i * U + (u + 1))
                act.nop().then_inc(self.sc_free, 1)
                act.wait_ge(self.out_done, i * U + (u + 1))
                act.activation(self.pT[:, u % 2, :, :], self.TP[:, :, :], ACT.Copy).then_inc(self.evacuated, 1)
                act.wait_ge(self.evacuated, i * U + (u + 1))
                act.nop().then_inc(self.tp_free, 1)

    def dve_steps(self):
        U, M = self.units, self.maps
        return U * M * (0 if self.bias is not None else 1) + U * (2 if M == 2 else 0) + U

    def dve(self, dve, i, step, out, bias=None, minus_lam=None):
        U, M = self.units, self.maps
        for u in range(-1, U + 1):
            if u + 1 < U:
                dve.wait_ge(self.sc_free, i * U + (u + 2))
                for mp in range(M):
                    n = (u + 1) * M + mp
                    dve.wait_ge(self.scored, i * (U * M) + (n + 1))
                    nm = self.nm[:, n % self.n_sc:n % self.n_sc + 1]
                    if self.bias is not None:
                        dve.memset(self.wait_taker[:], 0.0)
                        dve.tensor_tensor_reduce(out=self.sc[:, n % self.n_sc, :], in0=self.score_view(n),
                                                 in1=bias(u + 1), scale=-self.scale, scalar=-LOWEST,
                                                 op0=ALU.add, op1=ALU.min, accum_out=nm).then_inc(self.shifted, 1)
                        dve.wait_ge(self.shifted, i * (U * M) + (n + 1))
                        dve.nop().then_inc(self.s_free, 1)
                    else:
                        step(dve.tensor_reduce(nm, self.score_view(n), AX.X, ALU.max, negate=True))
                        dve.tensor_scalar(nm, nm, self.scale, None, ALU.mult).then_inc(self.shifted, 1)
            if M == 2 and 0 <= u < U:
                n = u * M
                dve.wait_ge(self.exped, i * (U * M) + (n + 2))
                c = n % (4 * M)
                step(dve.reciprocal(self.ri[:, c:c + 2], self.rs[:, c:c + 2]))
                a, b = self.sc[:, n % self.n_sc, :], self.sc[:, (n + 1) % self.n_sc, :]
                step(dve.tensor_scalar(b, b, self.ri[:, c + 1:c + 2], minus_lam, ALU.mult, ALU.mult))
                dve.scalar_tensor_tensor(a, a, self.ri[:, c:c + 1], b, ALU.mult, ALU.add).then_inc(self.mixed, 1)
            if u >= 1:
                w = u - 1
                dve.wait_ge(self.pv_done, i * U + (w + 1))
                dst = out(w)
                src = self.O[:, w % 2, 0:dst.shape[-1]]
                if M == 2:
                    step(dve.nop())
                    dve.tensor_copy(dst, src).then_inc(self.out_done, 1)
                else:
                    c = w % 4
                    step(dve.reciprocal(self.ri[:, c:c + 1], self.rs[:, c:c + 1]))
                    dve.tensor_scalar(dst, src, self.ri[:, c:c + 1], None, ALU.mult).then_inc(self.out_done, 1)


def pair_attention(nc, m, kind, weights, turns):
    with Stage(nc, kind) as st:
        WIDE = 3 * P
        biased = kind in ("diff", "even")
        maps = 2 if kind == "diff" else 1
        units = NT * (1 if kind == "diff" else 2)
        att = Attention(st, units, maps, 0.125, bias=True if biased else None)
        w = st.sb("w", [P, KD, WIDE])
        qkv = st.sb("qkv", [P, NT, WIDE])
        qT, kT = st.sb("qT", [P, S]), st.sb("kT", [P, S])
        w_in, par_in, bias_in, proj_done, proj_used, raw_in, qk_ready, qk_turned, qk_in, root_in, root, stepped = (
            st.sem(x) for x in ("w_in", "par_in", "bias_in", "proj_done", "proj_used", "raw_in", "qk_ready",
                                "qk_turned", "qk_in", "root_in", "root", "stepped"))
        n_par = 0
        params = []

        def param(name, src, shape):
            nonlocal n_par
            t = st.sb(name, shape)
            params.append((t, src))
            n_par += 16
            return t
        if biased:
            table = st.sb("table", [P, 1920])
        if kind == "even":
            params.append((table[:], m["dilated"]))
            n_par += 16
            cos, sin = param("cos", m["cos_even"], [P, NT * 8]), param("sin", m["sin_even"], [P, NT * 8])
            tmp = st.sb("tmp", [P, 4, NT * 4 * 8])
        if kind == "gqa":
            trig = [param(f"t{j}", src, [P, NT * 16]) for j, src in
                    enumerate((m["cos_row"], m["sin_row"], m["cos_col"], m["sin_col"]))]
            gq, gk = param("gq", m["odd_dq_norm_2"], [P, 64]), param("gk", m["odd_dk_norm_2"], [P, 64])
            tmp = st.sb("tmp", [P, 4, NT * 4 * 16])
            ss = st.sb("ss", [P, NT, 4])
        if kind == "diff":
            lp = param("lp", m["diff_lambda"], [P, 256])
            g_sub = param("g_sub", m["diff_subln_g"], [P, P])
            lam = st.sb("lam", [P, 4])
            lprod = st.sb("lprod", [P, 2, 64])
            ss = st.sb("ss", [P, NT * 4])
        block = st.block()

        @block.sync
        def _(sp):
            for t, src in params:
                sp.dma_start(t[:] if not isinstance(t, bass.AP) else t, src).then_inc(par_in, 16)
            m["ring"].feed(sp)

        @block.gpsimd
        def _(pool):
            def load(row):
                pool.dma_start(w[:, :, :], weights[row, :, :].rearrange("o p n -> (o p) n")).then_inc(w_in, 16)
            load(bass.ds(0, 1))
            if kind == "diff":
                pool.dma_start(table[:], m["alibi"][0, :, :]).then_inc(bias_in, 16)
            with pool.Fori(0, turns - 1) as i:
                pool.wait_ge(proj_done, i * NT + NT)
                load(bass.ds(i + 1, 1))
                if kind == "diff":
                    pool.wait_ge(att.shifted, i * (units * maps) + units * maps)
                    pool.dma_start(table[:], m["alibi"][bass.ds(i + 1, 1), :, :].rearrange("o p n -> (o p) n"))\
                        .then_inc(bias_in, 16)

        @block.tensor
        def _(pe):
            with pe.Fori(0, turns) as i:
                pe.wait_ge(w_in, i * 16 + 16)
                for t in range(NT):
                    if t >= 4:
                        pe.wait_ge(proj_used, i * NT + (t - 3))
                    for k in range(KD):
                        ins = pe.matmul(att.S[:, t % 4, 0:WIDE], m["hT"][:, k, t * P:(t + 1) * P], w[:, k, :],
                                        start=k == 0, stop=k == KD - 1)
                    ins.then_inc(proj_done, 1)
                pe.wait_ge(qk_ready, i + 1)
                for j in range(2):
                    for t in range(NT):
                        ins = pe.transpose(att.S[:, 2 * j + t // 4, (t % 4) * P:(t % 4 + 1) * P],
                                           qkv[:, t, j * P:(j + 1) * P], m["ident"][:])
                    ins.then_inc(qk_turned, 1)
                pe.wait_ge(qk_in, i * 2 + 2)
                if kind == "diff":
                    att.pe(pe, i, lambda u, mp: qT[64 * mp:64 * mp + 64, u * P:(u + 1) * P],
                           lambda u, mp: kT[64 * mp:64 * mp + 64, :], lambda u: qkv[:, :, 2 * P:3 * P], m["ident"][:])
                else:
                    def rows(u):
                        return slice(64 * (u // NT), 64 * (u // NT) + 64)
                    att.pe(pe, i, lambda u, mp: qT[rows(u), (u % NT) * P:(u % NT + 1) * P],
                           lambda u, mp: kT[rows(u), :],
                           lambda u: qkv[:, :, 2 * P + 64 * (u // NT):2 * P + 64 * (u // NT) + 64], m["ident"][:])

        @block.scalar
        def _(act):
            if kind == "diff":
                act.wait_ge(root_in, 1)
                act.activation(lam[:, 0:2], lam[:, 0:2], ACT.Exp).then_inc(root, 1)
            att.begin_act(act)
            with act.Fori(0, turns) as i:
                for t in range(NT):
                    act.wait_ge(proj_done, i * NT + (t + 1))
                    act.activation(qkv[:, t, :], att.S[:, t % 4, 0:WIDE], ACT.Copy).then_inc(proj_used, 1)
                if kind == "gqa":
                    act.wait_ge(root_in, i + 1)
                    act.activation(ss[:, :, :], ss[:, :, :], ACT.Sqrt).then_inc(root, 1)
                act.wait_ge(qk_turned, i * 2 + 1)
                act.activation(qT[:], att.S[:, 0:2, :].rearrange("p a n -> p (a n)"), ACT.Copy).then_inc(qk_in, 1)
                att.act(act, i)
            if kind == "diff":
                act.wait_ge(root_in, 2)
                act.activation(ss[:], ss[:], ACT.Sqrt).then_inc(root, 1)

        @block.vector
        def _(dve):
            step = Steps(dve, stepped)
            dve.wait_ge(par_in, n_par)
            att.begin_dve(dve)
            if kind == "diff":
                l4 = lp[:, :].rearrange("p (a c) -> p a c", c=64)
                for a in range(2):
                    dve.tensor_tensor(lprod[:, a, :], l4[:, 2 * a, :], l4[:, 2 * a + 1, :], ALU.mult)
                step(dve.nop())
                step(dve.tensor_copy(lam[:, 2:4], lp[:, 0:2]))
                dve.tensor_reduce(lam[:, 0:2], lprod[:, :, :], AX.X, ALU.add).then_inc(root_in, 1)
                dve.wait_ge(root, 1)
                step(dve.tensor_tensor(lam[:, 2:3], lam[:, 1:2], lam[:, 0:1], ALU.subtract))
                step(dve.tensor_scalar(lam[:, 2:3], lam[:, 2:3], -LAM_INIT, None, ALU.add))
            per = att.dve_steps() + {"diff": 0, "even": 2, "gqa": 10}[kind]
            with dve.Fori(0, turns) as i:
                step.turn(i, per)
                dve.wait_ge(proj_used, i * NT + NT)
                x = qkv[:, :, 0:2 * P].rearrange("p t (g c) -> p t g c", c=64)
                if kind == "diff":
                    dve.nop().then_inc(qk_ready, 1)
                    dve.wait_ge(bias_in, i * 16 + 16)
                if kind == "even":
                    shape = [P, NT, 4, 8]
                    c4, s4 = (v[:, :].rearrange("p (t c) -> p t c", c=8).unsqueeze(2).to_broadcast(shape)
                              for v in (cos, sin))
                    tm = [tmp[:, j, :].rearrange("p (t g c) -> p t g c", t=NT, g=4) for j in range(4)]
                    rope(step, dve, x[:, :, :, 0:8], x[:, :, :, 8:16], c4, s4, tm)
                    dve.nop().then_inc(qk_ready, 1)
                if kind == "gqa":
                    sq = tmp[:, :, :].rearrange("p a n -> p (a n)").rearrange("p (t g c) -> p t g c", t=NT, g=4)
                    group_squares(step, dve, x, sq, ss[:, :, :])
                    dve.tensor_scalar(ss[:, :, :], ss[:, :, :], 1.0 / 64, EPS, ALU.mult, ALU.add).then_inc(root_in, 1)
                    dve.wait_ge(root, i + 1)
                    step(dve.reciprocal(ss[:, :, :], ss[:, :, :]))
                    step(dve.tensor_tensor(x, x, ss[:, :, :].unsqueeze(3).to_broadcast([P, NT, 4, 64]), ALU.mult))
                    for half, g in ((slice(0, 2), gq), (slice(2, 4), gk)):
                        gb = g[:, :].unsqueeze(1).unsqueeze(1).to_broadcast([P, NT, 2, 64])
                        step(dve.tensor_tensor(x[:, :, half, :], x[:, :, half, :], gb, ALU.mult))
                    shape = [P, NT, 4, 16]
                    for a in range(2):
                        c4, s4 = (v[:, :].rearrange("p (t c) -> p t c", c=16).unsqueeze(2).to_broadcast(shape)
                                  for v in trig[2 * a:2 * a + 2])
                        tm = [tmp[:, j, :].rearrange("p (t g c) -> p t g c", t=NT, g=4) for j in range(4)]
                        rope(step, dve, x[:, :, :, 32 * a:32 * a + 16], x[:, :, :, 32 * a + 16:32 * a + 32], c4, s4, tm)
                    dve.nop().then_inc(qk_ready, 1)
                dve.wait_ge(qk_turned, i * 2 + 2)
                dve.tensor_copy(kT[:], att.S[:, 2:4, :].rearrange("p a n -> p (a n)")).then_inc(qk_in, 1)

                def out(u):
                    if kind == "diff":
                        return m["oN"][:, u, bass.ds(i * P, P)]
                    base = 512 if kind == "gqa" else 0
                    return m["oN"][:, u % NT, bass.ds(i * P + (base + 64 * (u // NT)), 64)]

                def bias(u):
                    c = 896 - P * (u % NT)
                    return table[:, c:c + S]
                att.dve(dve, i, step, out, bias=bias if biased else None,
                        minus_lam=lam[:, 2:3] if kind == "diff" else None)
            step.turned(turns)
            if kind == "diff":
                dve.wait_ge(att.out_done, 2 + turns * units)
                sq = att.sc[:, 0:4, :].rearrange("p a n -> p (a n)").rearrange("p (t g c) -> p t g c", g=4, c=P)
                o = m["oN"][:, :, 0:4 * P].rearrange("p t (g c) -> p t g c", c=P)
                s2 = ss[:, :].rearrange("p (t g) -> p t g", g=4)
                group_squares(step, dve, o, sq, s2)
                dve.tensor_scalar(ss[:], ss[:], 1.0 / P, EPS, ALU.mult, ALU.add).then_inc(root_in, 1)
                dve.wait_ge(root, 2)
                step(dve.reciprocal(ss[:], ss[:]))
                step(dve.tensor_tensor(sq, o, s2.unsqueeze(3).to_broadcast([P, NT, 4, P]), ALU.mult))
                step(dve.tensor_scalar(g_sub[:], g_sub[:], 1.0 - LAM_INIT, None, ALU.mult))
                step(dve.tensor_tensor(o, sq, g_sub[:, :].unsqueeze(1).unsqueeze(1).to_broadcast([P, NT, 4, P]),
                                       ALU.mult))


LAM_INIT = 0.8 - 0.6


def mla_attention(nc, m):
    with Stage(nc, "mla") as st:
        HEADS, QR, KR, RO, WIDE = 8, 256, 128, 32, 256
        first = m["ring"].take(1)
        att = Attention(st, NT, 1, 96.0 ** -0.5)
        low = st.sb("low", [P, NT, QR + KR + RO])
        cT = st.sb("cT", [P, 3, S])
        w = st.sb("w", [P, 2 * 96 + P])
        qkv = st.sb("qkv", [P, NT, WIDE])
        qT, kT = st.sb("qT", [96, S]), st.sb("kT", [96, S])
        cos, sin = st.sb("cos", [P, NT * 16]), st.sb("sin", [P, NT * 16])
        gq, gk = st.sb("gq", [P, QR]), st.sb("gk", [P, KR])
        tmp = st.sb("tmp", [P, 4, NT, 16])
        sq = st.sb("sq", [P, NT, QR])
        ss = st.sb("ss", [P, 2, NT])
        w_in, par_in, low_done, low_in, root_in, root, low_ready, low_turned, low_T, proj_done, proj_used, \
            qk_ready, qk_turned, qk_in, stepped = (
                st.sem(x) for x in ("w_in", "par_in", "low_done", "low_in", "root_in", "root", "low_ready",
                                    "low_turned", "low_T", "proj_done", "proj_used", "qk_ready", "qk_turned",
                                    "qk_in", "stepped"))
        block = st.block()

        @block.sync
        def _(sp):
            for t, src in ((cos, m["cos_mla"]), (sin, m["sin_mla"]), (gq, m["odd_cq_norm_2"]), (gk, m["odd_ckv_norm_2"])):
                sp.dma_start(t[:], src).then_inc(par_in, 16)
            m["ring"].feed(sp)

        @block.gpsimd
        def _(pool):
            pool.dma_start(w[:], m["w_mla"][0, :, :]).then_inc(w_in, 16)
            with pool.Fori(0, HEADS - 1) as i:
                pool.wait_ge(proj_done, i * NT + NT)
                pool.dma_start(w[:], m["w_mla"][bass.ds(i + 1, 1), :, :].rearrange("o p n -> (o p) n")).then_inc(w_in, 16)

        @block.tensor
        def _(pe):
            m["ring"].wait(pe, first)
            wl = m["ring"].slot(first, KD, QR + KR + RO)
            for t in range(NT):
                if t >= 4:
                    pe.wait_ge(low_in, t - 3)
                for k in range(KD):
                    ins = pe.matmul(att.S[:, t % 4, 0:QR + KR + RO], m["hT"][:, k, t * P:(t + 1) * P], wl[:, k, :],
                                    start=k == 0, stop=k == KD - 1)
                ins.then_inc(low_done, 1)
            pe.wait_ge(low_ready, 1)
            for j in range(3):
                if j == 2:
                    pe.wait_ge(low_T, 1)
                for t in range(NT):
                    ins = pe.transpose(att.S[:, 2 * (j % 2) + t // 4, (t % 4) * P:(t % 4 + 1) * P],
                                       low[:, t, j * P:(j + 1) * P], m["ident"][:])
                ins.then_inc(low_turned, 1)
            pe.wait_ge(low_T, 3)
            with pe.Fori(0, HEADS) as i:
                pe.wait_ge(w_in, i * 16 + 16)
                for t in range(NT):
                    if t >= 4:
                        pe.wait_ge(proj_used, i * NT + (t - 3))
                    for k in range(2):
                        pe.matmul(att.S[:, t % 4, 0:96], cT[:, k, t * P:(t + 1) * P], w[:, k * 96:(k + 1) * 96],
                                  start=k == 0, stop=k == 1)
                    pe.matmul(att.S[:, t % 4, 96:96 + P], cT[:, 2, t * P:(t + 1) * P], w[:, 192:192 + P],
                              start=True, stop=True).then_inc(proj_done, 1)
                pe.wait_ge(qk_ready, i + 1)
                for j in range(2):
                    for t in range(NT):
                        ins = pe.transpose(att.S[0:96, 2 * j + t // 4, (t % 4) * P:(t % 4 + 1) * P],
                                           qkv[:, t, j * 96:(j + 1) * 96], m["ident"][:])
                    ins.then_inc(qk_turned, 1)
                pe.wait_ge(qk_in, i * 2 + 2)
                att.pe(pe, i, lambda u, mp: qT[:, u * P:(u + 1) * P], lambda u, mp: kT[:, :],
                       lambda u: qkv[:, :, 192:256], m["ident"][:])

        @block.scalar
        def _(act):
            for t in range(NT):
                act.wait_ge(low_done, t + 1)
                act.activation(low[:, t, :], att.S[:, t % 4, 0:QR + KR + RO], ACT.Copy).then_inc(low_in, 1)
            m["ring"].release(act)
            act.wait_ge(root_in, 1)
            act.activation(ss[:, :, :], ss[:, :, :], ACT.Sqrt).then_inc(root, 1)
            for j in range(3):
                act.wait_ge(low_turned, j + 1)
                b = 2 * (j % 2)
                act.activation(cT[:, j, :], att.S[:, b:b + 2, :].rearrange("p a n -> p (a n)"), ACT.Copy)\
                   .then_inc(low_T, 1)
            att.begin_act(act)
            with act.Fori(0, HEADS) as i:
                for t in range(NT):
                    act.wait_ge(proj_done, i * NT + (t + 1))
                    act.activation(qkv[:, t, 0:160], att.S[:, t % 4, 0:160], ACT.Copy)
                    act.activation(qkv[:, t, 192:256], att.S[:, t % 4, 160:224], ACT.Copy).then_inc(proj_used, 1)
                act.wait_ge(qk_turned, i * 2 + 1)
                act.activation(qT[:], att.S[0:96, 0:2, :].rearrange("p a n -> p (a n)"), ACT.Copy).then_inc(qk_in, 1)
                att.act(act, i)

        @block.vector
        def _(dve):
            step = Steps(dve, stepped)
            dve.wait_ge(par_in, 64)
            att.begin_dve(dve)
            dve.wait_ge(low_in, NT)
            cq, ckv = low[:, :, 0:QR], low[:, :, QR:QR + KR]
            group_squares(step, dve, cq, sq[:, :, :], ss[:, 0, :])
            group_squares(step, dve, ckv, sq[:, :, 0:KR], ss[:, 1, :])
            step(dve.tensor_scalar(ss[:, 0, :], ss[:, 0, :], 1.0 / QR, EPS, ALU.mult, ALU.add))
            dve.tensor_scalar(ss[:, 1, :], ss[:, 1, :], 1.0 / KR, EPS, ALU.mult, ALU.add).then_inc(root_in, 1)
            dve.wait_ge(root, 1)
            step(dve.reciprocal(ss[:, :, :], ss[:, :, :]))
            step(dve.tensor_tensor(cq, cq, ss[:, 0, :].unsqueeze(2).to_broadcast([P, NT, QR]), ALU.mult))
            step(dve.tensor_tensor(cq, cq, gq[:, :].unsqueeze(1).to_broadcast([P, NT, QR]), ALU.mult))
            step(dve.tensor_tensor(ckv, ckv, ss[:, 1, :].unsqueeze(2).to_broadcast([P, NT, KR]), ALU.mult))
            dve.tensor_tensor(ckv, ckv, gk[:, :].unsqueeze(1).to_broadcast([P, NT, KR]), ALU.mult)\
               .then_inc(low_ready, 1)
            c3, s3 = (v[:, :].rearrange("p (t c) -> p t c", c=16) for v in (cos, sin))
            tm = [tmp[:, j, :, :] for j in range(4)]
            o = QR + KR
            rope(step, dve, low[:, :, o:o + 16], low[:, :, o + 16:o + 32], c3, s3, tm)
            step(dve.tensor_copy(qkv[:, :, 160:192], low[:, :, o:o + 32]))
            with dve.Fori(0, HEADS) as i:
                step.turn(i, att.dve_steps() + 2)
                dve.wait_ge(proj_used, i * NT + NT)
                rope(step, dve, qkv[:, :, 64:80], qkv[:, :, 80:96], c3, s3, tm)
                dve.nop().then_inc(qk_ready, 1)
                dve.wait_ge(qk_turned, i * 2 + 2)
                dve.tensor_copy(kT[:], att.S[0:96, 2:4, :].rearrange("p a n -> p (a n)")).then_inc(qk_in, 1)
                att.dve(dve, i, step, lambda u: m["oN"][:, u, bass.ds(i * 64, 64)])
            step.turned(HEADS)


def turn_over(pe, psum, src, ident, done, free):
    for t in range(NT):
        if t >= 2:
            pe.wait_ge(free, t - 1)
        for k in range(KD):
            ins = pe.transpose(psum[:, t % 2, k, :], src[:, t, k * P:(k + 1) * P], ident)
        ins.then_inc(done, 1)


def take_turned(act, psum, dst, done, free):
    for t in range(NT):
        act.wait_ge(done, t + 1)
        act.activation(dst[:, :, t * P:(t + 1) * P], psum[:, t % 2, :, :], ACT.Copy).then_inc(free, 1)


def merge_stage(nc, m):
    with Stage(nc, "merge") as st:
        first = m["ring"].take(8)
        oT = st.sb("oT", [P, KD, S])
        sig = st.sb("sig", [P, 2, HALF])
        prod = st.sb("prod", [P, HALF])
        tp = st.ps("tp", [P, 2, KD, P])
        G, U = st.ps("gate", [P, 2, HALF]), st.ps("up", [P, 2, HALF])
        turned, taken, g_done, g_free, u_done, u_free, sig_done, sig_free, stepped = (
            st.sem(x) for x in ("turned", "taken", "g_done", "g_free", "u_done", "u_free", "sig_done", "sig_free",
                                "stepped"))
        block = st.block()
        ROWS = (range(0, 4), range(4, 6), range(6, 8))
        N = 3 * NT

        @block.sync
        def _(sp):
            m["ring"].feed(sp)

        @block.tensor
        def _(pe):
            turn_over(pe, tp, m["oN"], m["ident"][:], turned, taken)
            pe.wait_ge(taken, NT)
            with pe.Fori(0, 2) as i:
                up = m["ring"].slot(first + 3, KD, HALF)
                for b in range(3):
                    wg = m["ring"].slot(first + b, KD, HALF)
                    m["ring"].wait(pe, first + b, i, 4)
                    for t in range(NT):
                        n = b * NT + t
                        pe.wait_ge(g_free, i * N + (n + 1))
                        for k in range(KD):
                            ins = pe.matmul(G[:, n % 2, :], m["hT"][:, k, t * P:(t + 1) * P], wg[:, k, :],
                                            start=k == 0, stop=k == KD - 1)
                        ins.then_inc(g_done, 1)
                        if n == 0:
                            m["ring"].wait(pe, first + 3, i, 4)
                        pe.wait_ge(u_free, i * N + (n + 1))
                        for k in ROWS[b]:
                            ins = pe.matmul(U[:, n % 2, :], oT[:, k, t * P:(t + 1) * P], up[:, k, :],
                                            start=k == ROWS[b][0], stop=k == ROWS[b][-1])
                        ins.then_inc(u_done, 1)

        @block.scalar
        def _(act):
            take_turned(act, tp, oT, turned, taken)
            start(act, g_free)
            with act.Fori(0, 2) as i:
                for n in range(N):
                    act.wait_ge(g_done, i * N + (n + 1))
                    if n % NT == NT - 1:
                        m["ring"].release(act)
                    act.wait_ge(sig_free, i * N + (n + 1))
                    act.activation(sig[:, n % 2, :], G[:, n % 2, :], ACT.Sigmoid).then_inc(sig_done, 1)
                    act.wait_ge(sig_done, i * N + (n + 1))
                    act.nop().then_inc(g_free, 1)

        @block.vector
        def _(dve):
            step = Steps(dve, stepped)
            start(dve, u_free, sig_free)
            with dve.Fori(0, 2) as i:
                step.turn(i, N + 2 * NT)
                for n in range(N):
                    b, t = n // NT, n % NT
                    dst = m["oN"][:, t, bass.ds(i * HALF, HALF)]
                    dve.wait_ge(sig_done, i * N + (n + 1))
                    dve.wait_ge(u_done, i * N + (n + 1))
                    if n == N - 1:
                        m["ring"].release(dve)
                    if b == 0:
                        step(dve.tensor_tensor(dst, sig[:, n % 2, :], U[:, n % 2, :], ALU.mult))
                    else:
                        step(dve.tensor_tensor(prod[:], sig[:, n % 2, :], U[:, n % 2, :], ALU.mult))
                    dve.nop().then_inc(u_free, 1)
                    dve.nop().then_inc(sig_free, 1)
                    if b:
                        step(dve.tensor_tensor(dst, dst, prod[:], ALU.add))
            step.turned(2)


def out_stage(nc, m, name, src, gate=None):
    with Stage(nc, name) as st:
        first = m["ring"].take(2)
        x = st.sb("x", [P, NT, D])
        gt = st.sb("gt", [P, D])
        y = st.sb("y", [P, 2, HALF])
        tp = st.ps("tp", [P, 2, KD, P])
        Y = st.ps("y_ps", [P, 4, HALF])
        x_in, g_in, turned, taken, done, free, stepped, added, stored = (
            st.sem(s) for s in ("x_in", "g_in", "turned", "taken", "done", "free", "stepped", "added", "stored"))
        block = st.block()

        @block.sync
        def _(sp):
            sp.dma_start(x[:], src.rearrange("(t p) d -> p t d", p=P)).then_inc(x_in, 16)
            if gate is not None:
                sp.dma_start(gt[:], m["mod"][:, gate * D:(gate + 1) * D]).then_inc(g_in, 16)
            m["ring"].feed(sp)

        @block.gpsimd
        def _(pool):
            for t in range(NT):
                pool.wait_ge(added, NT + t + 1)
                pool.dma_start(m["x1"][t * P:(t + 1) * P, :], x[:, t, :]).then_inc(stored, 16)
            pool.wait_ge(stored, 16 * NT)

        @block.tensor
        def _(pe):
            turn_over(pe, tp, m["oN"], m["ident"][:], turned, taken)
            pe.wait_ge(taken, NT)
            for half in range(2):
                w = m["ring"].slot(first + half, KD, HALF)
                m["ring"].wait(pe, first + half)
                for t in range(NT):
                    n = half * NT + t
                    if n >= 4:
                        pe.wait_ge(free, n - 3)
                    for k in range(KD):
                        ins = pe.matmul(Y[:, n % 4, :], m["hT"][:, k, t * P:(t + 1) * P], w[:, k, :],
                                        start=k == 0, stop=k == KD - 1)
                    ins.then_inc(done, 1)

        @block.scalar
        def _(act):
            take_turned(act, tp, m["hT"], turned, taken)

        @block.vector
        def _(dve):
            dve.wait_ge(x_in, 16)
            if gate is not None:
                dve.wait_ge(g_in, 16)
            for n in range(2 * NT):
                half, t = n // NT, n % NT
                cols = slice(half * HALF, (half + 1) * HALF)
                dve.wait_ge(done, n + 1)
                if t == NT - 1:
                    m["ring"].release(dve)
                add = Y[:, n % 4, :]
                if gate is not None:
                    dve.tensor_tensor(y[:, n % 2, :], add, gt[:, cols], ALU.mult).then_inc(free, 1)
                    dve.wait_ge(free, n + 1)
                    dve.tensor_tensor(x[:, t, cols], x[:, t, cols], y[:, n % 2, :], ALU.add).then_inc(added, 1)
                else:
                    dve.tensor_tensor(x[:, t, cols], x[:, t, cols], add, ALU.add).then_inc(free, 1)
                    dve.wait_ge(free, n + 1)
                    dve.nop().then_inc(added, 1)


def mlp_load(m, sp, what, turn):
    sp.dma_start(m["ring"].buf[:, what, :], m["w_mlp"][turn, :, :].rearrange("o p n -> (o p) n"))\
      .then_inc(m["mlp_w_in"][what], 16)


def mlp_ahead(m):
    def first_loads(sp):
        for what in range(2):
            mlp_load(m, sp, what, bass.ds(what, 1))
    return first_loads


def mlp_stage(nc, m):
    with Stage(nc, "mlp") as st:
        TURNS, F = 8, 4
        buf, buf_r = m["ring"].buf, m["ring"].buf_r
        x = st.sb("x", [P, NT, D])
        gt = st.sb("gt", [P, D])
        y = st.sb("y", [P, 2, HALF])
        r = st.sb("relu", [P, 2, HALF])
        w_high = st.sb("w_high", [P, 2, SLOT], F32R)
        h_high = buf_r[:, 2:4, :].rearrange("p a n -> p (a n)").rearrange("p (k s) -> p k s", k=KD)
        h_low = m["hT_r"]
        u_high, u_low = m["oN_r"][:, 0:F, :], m["oN_r"][:, F:2 * F, :]
        w1 = [t.rearrange("p (k n) -> p k n", k=KD) for t in (w_high[:, 0, :], buf_r[:, 0, :])]
        w2 = [t.rearrange("p (k n) -> p k n", k=F) for t in (w_high[:, 1, :], buf_r[:, 1, :])]
        Z, Y = st.ps("z", [P, 4, HALF]), st.ps("y_ps", [P, 4, HALF])
        x_in, h_split, w_split, z_done, z_free, r_free, u_in, y_done, y_free, stepped, added, stored = (
            st.sem(s) for s in ("x_in", "h_split", "w_split", "z_done", "z_free", "r_free", "u_in", "y_done",
                                "y_free", "stepped", "added", "stored"))
        block = st.block()
        NZ, NY = 2 * F, 2 * NT

        @block.sync
        def _(sp):
            sp.dma_start(x[:], m["x1"].rearrange("(t p) d -> p t d", p=P)).then_inc(x_in, 16)
            sp.dma_start(gt[:], m["mod"][:, 5 * D:6 * D]).then_inc(x_in, 16)
            with sp.Fori(0, TURNS - 1) as i:
                sp.wait_ge(z_done, i * NZ + NZ)
                mlp_load(m, sp, 0, bass.ds(i * 2 + 2, 1))
                sp.wait_ge(y_done, i * NY + NY)
                mlp_load(m, sp, 1, bass.ds(i * 2 + 3, 1))

        @block.gpsimd
        def _(pool):
            for t in range(NT):
                pool.wait_ge(added, TURNS * NY - NT + t + 1)
                pool.dma_start(m["x1"][t * P:(t + 1) * P, :], x[:, t, :]).then_inc(stored, 16)
            pool.wait_ge(stored, 16 * NT)

        @block.tensor
        def _(pe):
            pe.wait_ge(h_split, 1)
            with pe.Fori(0, TURNS) as i:
                pe.wait_ge(w_split, i * 2 + 1)
                for n in range(NZ):
                    f, th = n // 2, n % 2
                    if n >= 4:
                        pe.wait_ge(z_free, i * NZ + (n - 3))
                    for k in range(KD):
                        cols, toks = slice(f * P, (f + 1) * P), slice(th * HALF, (th + 1) * HALF)
                        ins = three_passes(pe, Z[:, n % 4, :], [w[:, k, cols] for w in w1],
                                           [h[:, k, toks] for h in (h_high, h_low)], k == 0, k == KD - 1)
                    ins.then_inc(z_done, 1)
                pe.wait_ge(w_split, i * 2 + 2)
                for n in range(NY):
                    half, t = n // NT, n % NT
                    if n >= 4:
                        pe.wait_ge(y_free, i * NY + (n - 3))
                    for k in range(F):
                        if n == 0:
                            pe.wait_ge(u_in, i * NZ + (2 * k + 1))
                        if n == NT // 2 and k == 0:
                            pe.wait_ge(u_in, i * NZ + NZ)
                        toks, cols = slice(t * P, (t + 1) * P), slice(half * HALF, (half + 1) * HALF)
                        ins = three_passes(pe, Y[:, n % 4, :], [u[:, k, toks] for u in (u_high, u_low)],
                                           [w[:, k, cols] for w in w2], k == 0, k == F - 1)
                    ins.then_inc(y_done, 1)

        @block.scalar
        def _(act):
            with act.Fori(0, TURNS) as i:
                for n in range(NZ):
                    act.wait_ge(z_done, i * NZ + (n + 1))
                    act.wait_ge(r_free, i * NZ + (n + 1))
                    act.activation(r[:, n % 2, :], Z[:, n % 4, :], ACT.Relu).then_inc(z_free, 1)

        @block.vector
        def _(dve):
            step = Steps(dve, stepped)
            start(dve, r_free)
            split(step, dve, m["hT"][:, :, :], h_high, h_low[:, :, :]).then_inc(h_split, 1)
            dve.wait_ge(m["mlp_w_in"][0], 16)
            split(step, dve, buf[:, 0, :], w_high[:, 0, :], buf_r[:, 0, :]).then_inc(w_split, 1)
            dve.wait_ge(x_in, 32)

            def turn(i, more):
                for n in range(NZ):
                    f, th = n // 2, n % 2
                    dve.wait_ge(z_free, i * NZ + (n + 1))
                    toks = slice(th * HALF, (th + 1) * HALF)
                    step(dve.tensor_tensor(r[:, n % 2, :], r[:, n % 2, :], r[:, n % 2, :], ALU.mult))
                    split(step, dve, r[:, n % 2, :], u_high[:, f, toks], u_low[:, f, toks]).then_inc(u_in, 1)
                    dve.wait_ge(u_in, i * NZ + (n + 1))
                    dve.nop().then_inc(r_free, 1)
                    if n == NZ - 3:
                        dve.wait_ge(m["mlp_w_in"][1], i * 16 + 16)
                        split(step, dve, buf[:, 1, :], w_high[:, 1, :], buf_r[:, 1, :]).then_inc(w_split, 1)
                for n in range(NY):
                    half, t = n // NT, n % NT
                    cols = slice(half * HALF, (half + 1) * HALF)
                    dve.wait_ge(y_done, i * NY + (n + 1))
                    dve.tensor_tensor(y[:, n % 2, :], Y[:, n % 4, :], gt[:, cols], ALU.mult).then_inc(y_free, 1)
                    dve.wait_ge(y_free, i * NY + (n + 1))
                    dve.tensor_tensor(x[:, t, cols], x[:, t, cols], y[:, n % 2, :], ALU.add).then_inc(added, 1)
                    if n == NY - 4 and more:
                        dve.wait_ge(m["mlp_w_in"][0], i * 16 + 32)
                        split(step, dve, buf[:, 0, :], w_high[:, 0, :], buf_r[:, 0, :]).then_inc(w_split, 1)
                dve.wait_ge(added, i * NY + NY)

            with dve.Fori(0, TURNS - 1) as i:
                step.turn(i, 2 * NZ + 2)
                turn(i, True)
            step.turned(TURNS - 1)
            turn(TURNS - 1, False)


def spatial_stage(nc, m):
    with Stage(nc, "spatial") as st:
        G, C, W2 = 4, 64, 256
        first = m["ring"].take(1)
        z = st.sb("z", [P, NT, HALF])
        sq = st.sb("sq", [P, NT, W2])
        ss = st.sb("ss", [P, NT, G])
        gn, ws, bs = st.sb("gn", [P, W2]), st.sb("ws", [P, G * P]), st.sb("bs", [P, G])
        Z = st.ps("z_ps", [P, 4, HALF])
        M = st.ps("mixed", [P, 2, HALF])
        par_in, z_done, z_free, root_in, root, v_ready, mixed, gated, stepped = (
            st.sem(s) for s in ("par_in", "z_done", "z_free", "root_in", "root", "v_ready", "mixed", "gated",
                                "stepped"))
        block = st.block()

        @block.sync
        def _(sp):
            for t, src in ((gn, m["even_gmlp_norm_2"]), (ws, m["w_spatial"]), (bs, m["b_spatial"])):
                sp.dma_start(t[:], src).then_inc(par_in, 16)
            m["ring"].feed(sp)

        @block.tensor
        def _(pe):
            w = m["ring"].slot(first, KD, HALF)
            m["ring"].wait(pe, first)
            for t in range(NT):
                if t >= 4:
                    pe.wait_ge(z_free, t - 3)
                for k in range(KD):
                    ins = pe.matmul(Z[:, t % 4, :], m["hT"][:, k, t * P:(t + 1) * P], w[:, k, :],
                                    start=k == 0, stop=k == KD - 1)
                ins.then_inc(z_done, 1)
            pe.wait_ge(v_ready, 1)
            for g in range(G):
                if g >= 2:
                    pe.wait_ge(gated, g - 1)
                v = z[:, :, W2 + g * C:W2 + (g + 1) * C]
                pe.matmul(M[:, g % 2, :].rearrange("p (t c) -> p t c", c=C), ws[:, g * P:(g + 1) * P], v,
                          start=True, stop=True).then_inc(mixed, 1)

        @block.scalar
        def _(act):
            for t in range(NT):
                act.wait_ge(z_done, t + 1)
                act.activation(z[:, t, :], Z[:, t % 4, :], ACT.Gelu_apprx_tanh).then_inc(z_free, 1)
            m["ring"].release(act)
            act.wait_ge(root_in, 1)
            act.activation(ss[:, :, :], ss[:, :, :], ACT.Sqrt).then_inc(root, 1)

        @block.vector
        def _(dve):
            step = Steps(dve, stepped)
            dve.wait_ge(par_in, 48)
            dve.wait_ge(z_free, NT)
            v = z[:, :, W2:2 * W2].rearrange("p t (g c) -> p t g c", c=C)
            group_squares(step, dve, v, sq[:, :, :].rearrange("p t (g c) -> p t g c", c=C), ss[:, :, :])
            dve.tensor_scalar(ss[:, :, :], ss[:, :, :], 1.0 / C, EPS, ALU.mult, ALU.add).then_inc(root_in, 1)
            dve.wait_ge(root, 1)
            step(dve.reciprocal(ss[:, :, :], ss[:, :, :]))
            step(dve.tensor_tensor(v, v, ss[:, :, :].unsqueeze(3).to_broadcast([P, NT, G, C]), ALU.mult))
            dve.tensor_tensor(z[:, :, W2:2 * W2], z[:, :, W2:2 * W2],
                              gn[:, :].unsqueeze(1).to_broadcast([P, NT, W2]), ALU.mult).then_inc(v_ready, 1)
            for g in range(G):
                dve.wait_ge(mixed, g + 1)
                u = z[:, :, g * C:(g + 1) * C]
                dve.scalar_tensor_tensor(m["oN"][:, :, 768 + g * C:768 + (g + 1) * C],
                                         M[:, g % 2, :].rearrange("p (t c) -> p t c", c=C), bs[:, g:g + 1], u,
                                         ALU.add, ALU.mult).then_inc(gated, 1)


def scan_stage(nc, m, kind):
    MAX_NEG_LOGIT = 80.0
    with Stage(nc, kind) as st:
        hgrn = kind == "hgrn"
        HEADS, DK, turns = (2, 64, 2) if hgrn else (4, 32, 1)
        VW = HEADS * 64
        off = 512 if hgrn else 768
        NC, LEVELS = S // P, 8
        T = st.sb("T", [P, 3, S])
        vg = st.sb("vg", [P, NT, 2 * VW])
        c = st.sb("c", [P, 2, S])
        E = st.sb("E", [P, 2, S])
        KQ = st.sb("KQ", [P, 2, S])
        st_f, st_b = st.sb("state_f", [P, NC, VW]), st.sb("state_b", [P, NC, VW])
        states = (st_f, st_b)
        AT = m["oN"][:, :, 0:4 * P]
        dec = st.sb("dec", [P, 2, NC])
        ss = st.sb("ss", [P, NT, HEADS])
        masks = st.sb("masks", [P, LEVELS, P], U8)
        restart = st.sb("restart", [P, S], U8)
        own = st.sb("own", [P, VW])
        gn = st.sb("gn", [P, 64])
        wait_taker = st.sb("wait_taker", [P, 1])
        if hgrn:
            w = st.sb("w", [P, KD, 5 * P])
            lbx = st.sb("lbx", [P, 4])
            lb, om = st.sb("lb", [P, 4]), st.sb("om", [P, 4])
            lbt, omt = st.sb("lbt", [P, 2]), st.sb("omt", [P, 2])
        else:
            first = m["ring"].take(2)
            w2, b2 = st.sb("w2", [16, 2 * P]), st.sb("b2", [P, 2])
        A, B = st.ps("A", [P, 4, HALF]), st.ps("B", [P, 4, HALF])
        B8 = B[:, :, :].rearrange("p a n -> p (a n)")[:, 0:NC * VW].rearrange("p (c v) -> p c v", v=VW)
        (par_in, w_in, t_done, t_in, n_done, n_in, gate_mm, gate_in, mags, logs, neg_k, keys, spans, spans_e, kend,
         kt_turned, kn_in, kv_done, kv_used, qe_exp, inter_ready, inter_done, x_ready, x_exp, kq_ready, lev_done,
         sel_done, intra_done, out_done, root_in, root, stepped, acted, lb_in) = (
            st.sem(x) for x in (
                "par_in", "w_in", "t_done", "t_in", "n_done", "n_in", "gate_mm", "gate_in", "mags", "logs", "neg_k",
                "keys", "spans", "spans_e", "kend", "kt_turned", "kn_in", "kv_done", "kv_used", "qe_exp",
                "inter_ready", "inter_done", "x_ready", "x_exp", "kq_ready", "lev_done", "sel_done", "intra_done",
                "out_done", "root_in", "root", "stepped", "acted", "lb_in"))
        block = st.block()
        params = [(E[:, 0, :], m["levels"]), (E[:, 1, :], m["restart"]),
                  (own[:], m["own64"] if hgrn else m["own32"]), (gn[:], m["hgrn_norm_g"] if hgrn else m["gla_norm_g"])]
        params += [(lbx[:], m["lb_logits"])] if hgrn else [(w2[:], m["gate_w2"]), (b2[:], m["gate_b"])]
        NTU = 6 if hgrn else 8

        def turn_loop(eng, body):
            if turns == 1:
                body(0)
            else:
                with eng.Fori(0, turns) as i:
                    body(i)

        def chunks(ap):
            return ap.rearrange("p (c n) -> p c n", n=P)

        @block.sync
        def _(sp):
            for t, src in params:
                sp.dma_start(t, src).then_inc(par_in, 16)
            m["ring"].feed(sp)

        @block.gpsimd
        def _(pool):
            if hgrn:
                pool.dma_start(w[:].rearrange("p k n -> p (k n)"), m["w_hgrn"][0, :, :]).then_inc(w_in, 16)
                pool.wait_ge(n_done, NT)
                pool.dma_start(w[:].rearrange("p k n -> p (k n)"), m["w_hgrn"][1, :, :]).then_inc(w_in, 16)

        @block.tensor
        def _(pe):
            def body(i):
                if hgrn:
                    pe.wait_ge(w_in, i * 16 + 16)
                    wt, wn = w[:, :, 0:3 * P], w[:, :, 3 * P:5 * P]
                    cols = [(j * P, P) for j in range(3)]
                else:
                    m["ring"].wait(pe, first)
                    wt, wn = m["ring"].slot(first, KD, 288), m["ring"].slot(first + 1, KD, HALF)
                    cols = [(0, P), (P, P), (2 * P, 16), (2 * P + 16, 16)]
                for n in range(NTU):
                    o, width = cols[n // 2]
                    if n >= 4:
                        pe.wait_ge(t_in, i * NTU + (n - 3))
                    for k in range(KD):
                        ins = pe.matmul(A[0:width, n % 4, :], wt[:, k, o:o + width],
                                        m["hT"][:, k, (n % 2) * HALF:(n % 2 + 1) * HALF], start=k == 0, stop=k == KD - 1)
                    ins.then_inc(t_done, 1)
                if not hgrn:
                    m["ring"].wait(pe, first + 1)
                for t in range(NT):
                    if t >= 4:
                        pe.wait_ge(n_in, i * NT + (t - 3))
                    for k in range(KD):
                        ins = pe.matmul(B[:, t % 4, 0:2 * VW], m["hT"][:, k, t * P:(t + 1) * P], wn[:, k, :],
                                        start=k == 0, stop=k == KD - 1)
                    ins.then_inc(n_done, 1)
                if not hgrn:
                    pe.wait_ge(t_in, NTU)
                    pe.wait_ge(par_in, 16 * len(params))
                    for n in range(4):
                        pe.matmul(A[:, n, :], w2[:, (n // 2) * P:(n // 2 + 1) * P],
                                  KQ[0:16, n // 2, (n % 2) * HALF:(n % 2 + 1) * HALF], start=True, stop=True)\
                          .then_inc(gate_mm, 1)
                pe.wait_ge(n_in, i * NT + NT)
                for d in range(2):
                    pe.wait_ge(kend, i * 2 + (d + 1))
                    for t in range(NC):
                        ins = pe.transpose(A[:, 2 * d + t // 4, (t % 4) * P:(t % 4 + 1) * P],
                                           E[:, d, t * P:(t + 1) * P], m["ident"][:])
                    ins.then_inc(kt_turned, 1)
                for d in range(2):
                    pe.wait_ge(kn_in, i * 2 + (d + 1))
                    if d:
                        pe.wait_ge(kv_used, i * 2 + 1)
                    for t in range(NC):
                        ins = pe.matmul(B8[:, t, :], KQ[:, d, t * P:(t + 1) * P], vg[:, t, 0:VW], start=True, stop=True)
                    ins.then_inc(kv_done, 1)
                pe.wait_ge(inter_ready, i + 1)
                for t in range(NC):
                    pe.matmul(B8[:, t, :], E[:, 0, t * P:(t + 1) * P], st_f[:, t, :], start=True, stop=False)
                    ins = pe.matmul(B8[:, t, :], E[:, 1, t * P:(t + 1) * P], st_b[:, t, :], start=False, stop=True)
                ins.then_inc(inter_done, 1)
                for lv in range(LEVELS):
                    pe.wait_ge(kq_ready, i * LEVELS + (lv + 1))
                    right = T[:, 0, :] if lv == 0 else KQ[:, 1, :]
                    for h in range(HEADS):
                        n = lv * HEADS + h
                        if n >= 2:
                            pe.wait_ge(sel_done, i * (LEVELS * HEADS) + (n - 1))
                        r = slice(DK * h, DK * (h + 1))
                        for t in range(NC):
                            cc = slice(t * P, (t + 1) * P)
                            ins = pe.matmul(A[:, 2 * (n % 2) + t // 4, (t % 4) * P:(t % 4 + 1) * P],
                                            KQ[r, 0, cc], right[r, cc], start=True, stop=True)
                        ins.then_inc(lev_done, 1)
                pe.wait_ge(sel_done, i * (LEVELS * HEADS) + LEVELS * HEADS)
                for t in range(NC):
                    for h in range(HEADS):
                        ins = pe.matmul(B8[:, t, 64 * h:64 * h + 64], AT[:, t, h * P:(h + 1) * P],
                                        vg[:, t, 64 * h:64 * h + 64], start=True, stop=True)
                ins.then_inc(intra_done, 1)
                pe.wait_ge(out_done, i + 1)
            turn_loop(pe, body)

        @block.scalar
        def _(act):
            step = Steps(act, acted)
            if hgrn:
                act.wait_ge(lb_in, 1)
                act.activation(lb[:], lbx[:], ACT.Exp).then_inc(lb_in, 1)

            def body(i):
                step.turn(i, 5 if hgrn else 3)
                for n in range(NTU):
                    act.wait_ge(t_done, i * NTU + (n + 1))
                    j, hh = n // 2, slice((n % 2) * HALF, (n % 2 + 1) * HALF)
                    if hgrn:
                        act.activation(T[:, j, hh], A[:, n % 4, :], ACT.Silu if j == 0 else ACT.Copy).then_inc(t_in, 1)
                    elif j < 2:
                        act.activation(T[:, j, hh], A[:, n % 4, :], ACT.Copy).then_inc(t_in, 1)
                    else:
                        act.activation(KQ[0:16, j - 2, hh], A[0:16, n % 4, :], ACT.Copy).then_inc(t_in, 1)
                if not hgrn:
                    m["ring"].release(act)
                for t in range(NT):
                    act.wait_ge(n_done, i * NT + (t + 1))
                    act.activation(vg[:, t, 0:VW], B[:, t % 4, 0:VW], ACT.Copy)
                    act.activation(vg[:, t, VW:2 * VW], B[:, t % 4, VW:2 * VW], ACT.Silu).then_inc(n_in, 1)
                if not hgrn:
                    m["ring"].release(act)
                act.wait_ge(mags, i + 1)
                step(act.activation(E[:, :, :], E[:, :, :], ACT.Exp, scale=-1.0))
                if hgrn:
                    step(act.activation(KQ[:, :, :], KQ[:, :, :], ACT.Exp))
                    for d in range(2):
                        last = act.activation(KQ[:, d, :], KQ[:, d, :], ACT.Ln, bias=1.0, scale=lbt[:, d:d + 1])
                    step(last)
                act.activation(E[:, :, :], E[:, :, :], ACT.Ln, bias=1.0).then_inc(logs, 1)
                if hgrn:
                    act.wait_ge(neg_k, i + 1)
                    act.activation(T[:, 1:3, :], T[:, 1:3, :], ACT.Exp, scale=-1.0).then_inc(keys, 1)
                act.wait_ge(spans, i + 1)
                step(act.activation(E[:, :, :], E[:, :, :], ACT.Exp))
                act.activation(dec[:, :, :], dec[:, :, :], ACT.Exp).then_inc(spans_e, 1)
                for d in range(2):
                    act.wait_ge(kt_turned, i * 2 + (d + 1))
                    act.activation(KQ[:, d, :], A[:, 2 * d:2 * d + 2, :].rearrange("p a n -> p (a n)"), ACT.Copy)\
                       .then_inc(kn_in, 1)
                step(act.activation(E[:, :, :], c[:, :, :], ACT.Exp))
                act.nop().then_inc(qe_exp, 1)
                for lv in range(1, LEVELS):
                    act.wait_ge(x_ready, i * (LEVELS - 1) + lv)
                    act.activation(E[:, :, :], E[:, :, :], ACT.Exp).then_inc(x_exp, 1)
                act.wait_ge(root_in, i + 1)
                act.activation(ss[:, :, :], ss[:, :, :], ACT.Sqrt).then_inc(root, 1)
            turn_loop(act, body)
            step.turned(turns)

        @block.vector
        def _(dve):
            step = Steps(dve, stepped)
            dve.wait_ge(par_in, 16 * len(params))
            step(dve.tensor_copy(masks[:].rearrange("p l n -> p (l n)"), E[:, 0, :]))
            step(dve.tensor_copy(restart[:], E[:, 1, :]))
            if hgrn:
                dve.tensor_tensor(lbx[:], lbx[:], lbx[:], ALU.subtract).then_inc(lb_in, 1)
                dve.wait_ge(lb_in, 2)
                step(dve.reciprocal(om[:], lb[:]))
                step(dve.tensor_tensor(lb[:], lb[:], om[:], ALU.mult))
                step(dve.tensor_tensor(lb[:], lb[:], lb[:], ALU.subtract))
                step(dve.tensor_scalar(om[:], lb[:], -1.0, 1.0, ALU.mult, ALU.add))

            def body(i):
                step.turn(i, 37 if hgrn else 38)
                if hgrn:
                    dve.tensor_copy(lbt[:], lb[:, bass.ds(i * 2, 2)])
                    step(dve.tensor_copy(omt[:], om[:, bass.ds(i * 2, 2)]))
                    dve.wait_ge(t_in, i * NTU + NTU)
                    z = T[:, 1:3, :]
                    step(dve.tensor_scalar(T[:, 0, :], T[:, 0, :], 64 ** -0.5, None, ALU.mult))
                    dve.tensor_scalar(KQ[:, :, :], z, -1.0, MAX_NEG_LOGIT, ALU.mult, ALU.min)
                    kf, kb = T[:, 1, :], T[:, 2, :]
                else:
                    for n in range(4):
                        dve.wait_ge(gate_mm, n + 1)
                        step(dve.tensor_scalar(c[:, n // 2, (n % 2) * HALF:(n % 2 + 1) * HALF], A[:, n, :],
                                               b2[:, n // 2:n // 2 + 1], None, ALU.add))
                    step(dve.tensor_scalar(T[:, 0, :], T[:, 0, :], 32 ** -0.5, None, ALU.mult))
                    z = c[:, :, :]
                    kf = kb = T[:, 1, :]
                step(dve.scalar_tensor_tensor(E[:, :, :], z, -1.0, z, ALU.mult, ALU.max))
                dve.nop().then_inc(mags, 1)
                dve.wait_ge(logs, i + 1)
                if hgrn:
                    step(dve.scalar_tensor_tensor(KQ[:, :, :], z, 0.0, KQ[:, :, :], ALU.min, ALU.add))
                    step(dve.tensor_tensor(KQ[:, :, :], KQ[:, :, :], E[:, :, :], ALU.subtract))
                    dve.scalar_tensor_tensor(z, z, 0.0, E[:, :, :], ALU.max, ALU.add).then_inc(neg_k, 1)
                    la = KQ
                else:
                    step(dve.scalar_tensor_tensor(E[:, :, :], z, 0.0, E[:, :, :], ALU.min, ALU.subtract))
                    step(dve.tensor_scalar(E[:, :, :], E[:, :, :], 1.0 / 16.0, None, ALU.mult))
                    la = E
                dve.tensor_tensor_scan(c[:, 0, :], restart[:], la[:, 0, :], 0.0, ALU.mult, ALU.add)
                step(dve.tensor_tensor_scan(c[:, 1, ::-1], restart[:], la[:, 1, ::-1], 0.0, ALU.mult, ALU.add))
                ends = (chunks(c[:, 0, :])[:, :, P - 1:P], chunks(c[:, 1, :])[:, :, 0:1])
                for d in range(2):
                    dve.tensor_copy(dec[:, d, :].unsqueeze(2), ends[d])
                    last = dve.tensor_tensor(chunks(E[:, d, :]), ends[d].to_broadcast([P, NC, P]), chunks(c[:, d, :]),
                                             ALU.subtract)
                last.then_inc(spans, 1)
                if hgrn:
                    dve.wait_ge(keys, i + 1)
                    for d, k in ((0, kf), (1, kb)):
                        step(dve.tensor_scalar(k, k, omt[:, d:d + 1], None, ALU.mult))
                dve.wait_ge(spans_e, i + 1)
                for d, k in ((0, kf), (1, kb)):
                    dve.tensor_tensor(E[:, d, :], E[:, d, :], k, ALU.mult).then_inc(kend, 1)
                for d in range(2):
                    dve.wait_ge(kv_done, i * 2 + (d + 1))
                    s_ = states[d]
                    src, dst = (slice(0, NC - 1), slice(1, NC)) if d == 0 else (slice(1, NC), slice(0, NC - 1))
                    edge = 0 if d == 0 else NC - 1
                    dve.memset(s_[:, edge, :], 0.0)
                    dve.tensor_tensor(s_[:, dst, :], B8[:, src, :],
                                      own[:, :].unsqueeze(1).to_broadcast([P, NC - 1, VW]), ALU.mult)\
                       .then_inc(kv_used, 1)
                    dve.wait_ge(kv_used, i * 2 + (d + 1))
                    for n in range(1, NC - 1):
                        a, b = (n, n + 1) if d == 0 else (NC - 1 - n, NC - 2 - n)
                        step(dve.scalar_tensor_tensor(s_[:, b, :], s_[:, a, :], dec[:, d, a:a + 1], s_[:, b, :],
                                                      ALU.mult, ALU.add))
                dve.wait_ge(qe_exp, i + 1)
                step(dve.tensor_tensor(E[:, :, :], E[:, :, :], T[:, 0, :].unsqueeze(1).to_broadcast([P, 2, S]), ALU.mult))
                dve.nop().then_inc(inter_ready, 1)
                dst = m["oN"][:, :, bass.ds(i * P + off, VW)] if hgrn else m["oN"][:, :, off:off + VW]
                step(dve.tensor_tensor(KQ[:, 0, :], kf, kb, ALU.add))
                dve.nop().then_inc(kq_ready, 1)
                dve.wait_ge(inter_done, i + 1)
                step(dve.tensor_scalar(dst, B8[:, :, :], 1.0, None, ALU.mult))

                def halves(ap, size):
                    v = ap.rearrange("p (b n) -> p b n", n=size)
                    return v[:, :, 0:size // 2], v[:, :, size // 2:size]

                def exponents(lv):
                    size = 1 << lv
                    nb, hs = S // size, size // 2
                    shape = [P, nb, hs]
                    cf, cb = halves(c[:, 0, :], size), halves(c[:, 1, :], size)
                    rf = cf[0][:, :, hs - 1:hs].to_broadcast(shape)
                    rb = cb[1][:, :, 0:1].to_broadcast(shape)
                    xk, xq = halves(E[:, 0, :], size), halves(E[:, 1, :], size)
                    dve.tensor_tensor(xk[0], rf, cf[0], ALU.subtract)
                    dve.tensor_tensor(xk[1], rb, cb[1], ALU.subtract)
                    dve.tensor_tensor(xq[0], cb[0], rb, ALU.subtract)
                    dve.tensor_tensor(xq[1], cf[1], rf, ALU.subtract).then_inc(x_ready, 1)

                def select(lv):
                    for h in range(HEADS):
                        n = lv * HEADS + h
                        dve.wait_ge(lev_done, i * (LEVELS * HEADS) + (n + 1))
                        src = A[:, 2 * (n % 2):2 * (n % 2) + 2, :].rearrange("p a (c n) -> p (a c) n", n=P)
                        to = AT[:, :, h * P:(h + 1) * P]
                        dve.memset(wait_taker[:], 0.0)
                        if lv == 0:
                            dve.tensor_copy(to, src).then_inc(sel_done, 1)
                        else:
                            dve.copy_predicated(to, masks[:, lv, :].unsqueeze(1).to_broadcast([P, NC, P]), src)\
                               .then_inc(sel_done, 1)
                        dve.wait_ge(sel_done, i * (LEVELS * HEADS) + (n + 1))

                for lv in range(1, LEVELS):
                    exponents(lv)
                    select(lv - 1)
                    dve.wait_ge(x_exp, i * (LEVELS - 1) + lv)
                    size = 1 << lv
                    x, f, b, o = (halves(v, size) for v in (E[:, 0, :], kf, kb, KQ[:, 0, :]))
                    if hgrn:
                        dve.tensor_tensor(o[0], x[0], f[0], ALU.mult)
                        dve.tensor_tensor(o[1], x[1], b[1], ALU.mult)
                    else:
                        dve.tensor_tensor(KQ[:, 0, :], E[:, 0, :], kf, ALU.mult)
                    step(dve.tensor_tensor(KQ[:, 1, :], E[:, 1, :], T[:, 0, :], ALU.mult))
                    dve.nop().then_inc(kq_ready, 1)
                select(LEVELS - 1)
                dve.wait_ge(intra_done, i + 1)
                step(dve.tensor_tensor(dst, dst, B8[:, :, :], ALU.add))
                sq = KQ[:, :, :].rearrange("p a n -> p (a n)")[:, 0:NT * VW].rearrange("p (t v) -> p t v", v=VW)
                sqg = sq.rearrange("p t (g c) -> p t g c", c=64)
                step(dve.tensor_tensor(sq, dst, dst, ALU.mult))
                step(dve.tensor_reduce(ss[:, :, :], sqg, AX.X, ALU.add))
                dve.tensor_scalar(ss[:, :, :], ss[:, :, :], 1.0 / 64, EPS, ALU.mult, ALU.add).then_inc(root_in, 1)
                step(dve.tensor_tensor(sq, dst, vg[:, :, VW:2 * VW], ALU.mult))
                dve.wait_ge(root, i + 1)
                step(dve.reciprocal(ss[:, :, :], ss[:, :, :]))
                step(dve.tensor_tensor(sqg, sqg, ss[:, :, :].unsqueeze(3).to_broadcast([P, NT, HEADS, 64]), ALU.mult))
                step(dve.tensor_tensor(sqg, sqg, gn[:, :].unsqueeze(1).unsqueeze(1).to_broadcast([P, NT, HEADS, 64]),
                                       ALU.mult))
                dve.tensor_scalar(dst, sq, 1.0, None, ALU.mult).then_inc(out_done, 1)
                dve.wait_ge(out_done, i + 1)
            turn_loop(dve, body)
            step.turned(turns)


def moe_stage(nc, m, layer):
    with Stage(nc, f"moe{layer}") as st:
        NE, CAP, EJ, K4 = 16, P, 4, 4
        TURNS = NE // EJ
        first = m["ring"].take(3 * NE)
        wr = st.sb("wr", [P, KD, NE])
        aff = st.sb("aff", [P, NT, NE])
        mx = st.sb("mx", [P, NT])
        work = st.sb("work", [NE, S])
        vals, idx, idxf = st.sb("vals", [NE, CAP]), st.sb("idx", [NE, CAP], U32), st.sb("idxf", [NE, CAP])
        gates, rows = st.sb("gates", [P, NE]), st.sb("rows", [P, NE], U32)
        row = st.sb("row", [P, EJ], U32)
        xs, xT = st.sb("xs", [P, 2, D]), st.sb("xT", [P, 2, KD, P])
        sg, a, aT = st.sb("sg", [P, 2, HALF]), st.sb("a", [P, 2, HALF]), st.sb("aT", [P, 2, K4, P])
        y = st.sb("y", [P, 2, D])
        taker, zero, zeroed = st.sb("taker", [P, 2 * EJ]), st.sb("zero", [P, 1]), st.sem("zeroed")
        TP, AP_ = st.ps("xt_ps", [P, 4, P]), st.ps("at_ps", [P, 4, P])
        G, U, Y = st.ps("g_ps", [P, 2, HALF]), st.ps("u_ps", [P, 2, HALF]), st.ps("y_ps", [P, 2, HALF])
        (wr_in, logits, shifted, exped, aff_in, aff_T, work_in, topped, sel_T, sel_in, stepped, row_in, row_moved,
         xt_done, xt_in, tp_free, g_done, u_done, gu_free, sg_in, sg_free, a_in, at_done, at_in, at_free, y_done, y_free, y_in,
         added, y_gone) = (
            st.sem(x) for x in (
                "wr_in", "logits", "shifted", "exped", "aff_in", "aff_T", "work_in", "topped", "sel_T", "sel_in",
                "stepped", "row_in", "row_moved", "xt_done", "xt_in", "tp_free", "g_done", "u_done", "gu_free", "sg_in",
                "sg_free", "a_in", "at_done", "at_in", "at_free", "y_done", "y_free", "y_in", "added", "y_gone"))
        xs_in = [st.sem(f"xs_in{b}") for b in range(2)]
        block = st.block()
        L = G[:, 0, 0:NT * NE].rearrange("p (t e) -> p t e", e=NE)
        GU = U[0:NE, :, :].rearrange("p a n -> p (a n)")
        ids = m["ident"]

        @block.sync
        def _(sp):
            sp.dma_start(wr[:].rearrange("p k n -> p (k n)"), (m["w_router_0"], m["w_router_1"])[layer]).then_inc(wr_in, 16)
            m["ring"].feed(sp)

        @block.gpsimd
        def _(pool):
            pool.wait_ge(sel_in, 1)

            def take_wait(n):
                pool.tensor_tensor(taker[:, n:n + 1], zero[:], zero[:], ALU.add)

            pool.memset(zero[:], 0.0).then_inc(zeroed, 1)
            pool.wait_ge(zeroed, 1)

            def gather(i, j):
                b, r = j % 2, j % EJ
                if j >= 2:
                    pool.wait_ge(xt_in, i * (2 * EJ) + 2 * (j - 1))
                at = EJ * i + j
                pool.tensor_copy(row[:, r:r + 1], rows[:, bass.ds(at, 1)]).then_inc(row_moved, 1)
                pool.wait_ge(row_moved, at + 1)
                take_wait(r)
                pool.indirect_dma_start(xs[:, b, :], None, m["h"], bass.IndirectOffsetOnAxis(ap=row[:, r:r + 1], axis=0))\
                    .then_inc(xs_in[b], 16)

            start(pool, y_gone)
            for j in range(3):
                gather(0, j)

            def body(i, more):
                for j in range(EJ):
                    b = j % 2
                    if more or j + 3 < EJ:
                        gather(i, j + 3)
                    pool.wait_ge(y_in, i * (2 * EJ) + 2 * (j + 1))
                    take_wait(EJ + j)
                    pool.indirect_dma_start(m["x1"], bass.IndirectOffsetOnAxis(ap=row[:, j:j + 1], axis=0), y[:, b, :],
                                            None, compute_op=ALU.add).then_inc(added, 16)
                    pool.wait_ge(added, i * (16 * EJ) + 16 * (j + 1))
                    pool.nop().then_inc(y_gone, 1)
            per_turn(pool, TURNS, body)

        @block.tensor
        def _(pe):
            pe.wait_ge(wr_in, 16)
            for t in range(NT):
                for k in range(KD):
                    ins = pe.matmul(L[:, t, :], m["hT"][:, k, t * P:(t + 1) * P], wr[:, k, :], start=k == 0,
                                    stop=k == KD - 1)
            ins.then_inc(logits, 1)
            pe.wait_ge(aff_in, 1)
            for t in range(NT):
                ins = pe.transpose(GU[:, t * P:(t + 1) * P], aff[:, t, :], ids[:])
            ins.then_inc(aff_T, 1)
            pe.wait_ge(topped, 1)
            pe.transpose(TP[:, 0, 0:NE], vals[:, :], ids[0:NE, 0:NE])
            pe.transpose(TP[:, 1, 0:NE], idxf[:, :], ids[0:NE, 0:NE]).then_inc(sel_T, 1)
            pe.wait_ge(sel_in, 1)

            def turn_x(i, j, half):
                b = j % 2
                if half == 0:
                    pe.wait_ge(xs_in[b], i * (16 * EJ // 2) + 16 * (j // 2 + 1))
                pe.wait_ge(tp_free, i * (2 * EJ) + 2 * j + half + 1)
                for k in range(4):
                    kk = 4 * half + k
                    ins = pe.transpose(TP[:, k, :], xs[:, b, kk * P:(kk + 1) * P], ids[:])
                ins.then_inc(xt_done, 1)

            def product(i, j, what, done, g):
                w = m["ring"].slot(g, KD, HALF)
                m["ring"].wait(pe, g, i, 3 * EJ)
                if what is G:
                    pe.wait_ge(xt_in, i * (2 * EJ) + 2 * (j + 1))
                    pe.wait_ge(gu_free, i * EJ + (j + 1))
                for k in range(KD):
                    ins = pe.matmul(what[:, j % 2, :], xT[:, j % 2, k, :], w[:, k, :], start=k == 0, stop=k == KD - 1)
                ins.then_inc(done, 1)

            for half in range(2):
                turn_x(0, 0, half)
            product(0, 0, G, g_done, first)
            turn_x(0, 1, 0)
            product(0, 0, U, u_done, first + 1)
            turn_x(0, 1, 1)

            def body(i, more):
                g = first + 2
                for j in range(EJ):
                    nxt, after = more or j + 1 < EJ, more or j + 2 < EJ
                    if nxt:
                        product(i, j + 1, G, g_done, g)
                    if after:
                        turn_x(i, j + 2, 0)
                    pe.wait_ge(a_in, i * EJ + (j + 1))
                    pe.wait_ge(at_free, i * EJ + (j + 1))
                    for k in range(K4):
                        ins = pe.transpose(AP_[:, k, :], a[:, j % 2, k * P:(k + 1) * P], ids[:])
                    ins.then_inc(at_done, 1)
                    if nxt:
                        product(i, j + 1, U, u_done, g + 1)
                        g += 2
                    if after:
                        turn_x(i, j + 2, 1)
                    w = m["ring"].slot(g, K4, D)
                    m["ring"].wait(pe, g, i, 3 * EJ)
                    g += 1
                    pe.wait_ge(at_in, i * EJ + (j + 1))
                    for half in range(2):
                        pe.wait_ge(y_free, i * (2 * EJ) + 2 * j + half + 1)
                        for k in range(K4):
                            ins = pe.matmul(Y[:, half, :], aT[:, j % 2, k, :], w[:, k, half * HALF:(half + 1) * HALF],
                                            start=k == 0, stop=k == K4 - 1)
                        ins.then_inc(y_done, 1)
            per_turn(pe, TURNS, body)

        @block.scalar
        def _(act):
            act.wait_ge(shifted, 1)
            act.activation(aff[:, :, :], aff[:, :, :], ACT.Exp).then_inc(exped, 1)
            act.wait_ge(aff_T, 1)
            act.activation(work[:], GU, ACT.Copy).then_inc(work_in, 1)
            act.wait_ge(sel_in, 1)
            act.nop().then_inc(tp_free, 1)
            act.nop().then_inc(at_free, 1)

            def take_x(i, j, half):
                n = 2 * j + half
                act.wait_ge(xt_done, i * (2 * EJ) + n + 1)
                act.activation(xT[:, j % 2, 4 * half:4 * half + 4, :], TP[:, :, :], ACT.Copy).then_inc(xt_in, 1)
                act.wait_ge(xt_in, i * (2 * EJ) + n + 1)
                act.nop().then_inc(tp_free, 1)

            def gate(i, j):
                act.wait_ge(g_done, i * EJ + (j + 1))
                m["ring"].release(act)
                act.wait_ge(sg_free, i * EJ + (j + 1))
                act.activation(sg[:, j % 2, :], G[:, j % 2, :], ACT.Silu).then_inc(sg_in, 1)

            def up(i, j):
                act.wait_ge(u_done, i * EJ + (j + 1))
                m["ring"].release(act)

            for half in range(2):
                take_x(0, 0, half)
            gate(0, 0)
            take_x(0, 1, 0)
            up(0, 0)
            take_x(0, 1, 1)

            def body(i, more):
                for j in range(EJ):
                    nxt, after = more or j + 1 < EJ, more or j + 2 < EJ
                    if nxt:
                        gate(i, j + 1)
                    if after:
                        take_x(i, j + 2, 0)
                    act.wait_ge(at_done, i * EJ + (j + 1))
                    act.activation(aT[:, j % 2, :, :], AP_[:, :, :], ACT.Copy).then_inc(at_in, 1)
                    act.wait_ge(at_in, i * EJ + (j + 1))
                    act.nop().then_inc(at_free, 1)
                    if nxt:
                        up(i, j + 1)
                    if after:
                        take_x(i, j + 2, 1)
                    act.wait_ge(y_done, i * (2 * EJ) + 2 * (j + 1))
                    m["ring"].release(act)
            per_turn(act, TURNS, body)

        @block.vector
        def _(dve):
            step = Steps(dve, stepped)
            dve.wait_ge(logits, 1)
            step(dve.tensor_reduce(mx[:], L, AX.X, ALU.max))
            dve.tensor_tensor(aff[:, :, :], L, mx[:, :].unsqueeze(2).to_broadcast([P, NT, NE]), ALU.subtract)\
               .then_inc(shifted, 1)
            dve.wait_ge(exped, 1)
            step(dve.tensor_reduce(mx[:], aff[:, :, :], AX.X, ALU.add))
            step(dve.reciprocal(mx[:], mx[:]))
            dve.tensor_tensor(aff[:, :, :], aff[:, :, :], mx[:, :].unsqueeze(2).to_broadcast([P, NT, NE]), ALU.mult)\
               .then_inc(aff_in, 1)
            dve.wait_ge(work_in, 1)
            for r in range(CAP // 8):
                c8 = slice(8 * r, 8 * r + 8)
                step(dve.max(vals[:, c8], work[:]))
                step(dve.max_index(idx[:, c8], vals[:, c8], work[:]))
                if r + 1 < CAP // 8:
                    step(dve.match_replace(work[:], vals[:, c8], work[:], -1.0))
            dve.tensor_copy(idxf[:], idx[:]).then_inc(topped, 1)
            dve.wait_ge(sel_T, 1)
            dve.tensor_copy(gates[:], TP[:, 0, 0:NE])
            dve.tensor_copy(rows[:], TP[:, 1, 0:NE]).then_inc(sel_in, 1)
            dve.wait_ge(sel_in, 1)
            start(dve, gu_free, sg_free, y_free)

            def gated(i, j):
                dve.wait_ge(sg_in, i * EJ + (j + 1))
                dve.wait_ge(u_done, i * EJ + (j + 1))
                dve.tensor_tensor(a[:, j % 2, :], sg[:, j % 2, :], U[:, j % 2, :], ALU.mult).then_inc(a_in, 1)
                dve.wait_ge(a_in, i * EJ + (j + 1))
                dve.nop().then_inc(gu_free, 1)
                dve.nop().then_inc(sg_free, 1)

            gated(0, 0)

            def body(i, more):
                for j in range(EJ):
                    if more or j + 1 < EJ:
                        gated(i, j + 1)
                    dve.wait_ge(y_gone, i * EJ + (j + 1))
                    for half in range(2):
                        n = 2 * j + half
                        dve.wait_ge(y_done, i * (2 * EJ) + n + 1)
                        dve.tensor_scalar(y[:, j % 2, half * HALF:(half + 1) * HALF], Y[:, half, :],
                                          gates[:, bass.ds(EJ * i + j, 1)], None, ALU.mult).then_inc(y_in, 1)
                        dve.wait_ge(y_in, i * (2 * EJ) + n + 1)
                        dve.nop().then_inc(y_free, 1)
            per_turn(dve, TURNS, body)


def build_program(nc, m, out):
    with ExitStack() as ctx:
        m["mod"] = nc.dram_tensor("mod_rows", (P, 6 * D), F32, kind="Internal").ap()
        m["x1"] = nc.dram_tensor("x_rows", (S, D), F32, kind="Internal").ap()
        m["h"] = nc.dram_tensor("h_rows", (S, D), F32, kind="Internal").ap()
        m["ring"] = Ring(nc, ctx, m["w_all"])
        m["hT"], m["hT_r"] = twin_buffer(nc, ctx, "hT", [P, KD, S])
        m["oN"], m["oN_r"] = twin_buffer(nc, ctx, "oN", [P, NT, D])
        m["ident_dram"], m["ident"] = m["ident"], ctx.enter_context(nc.sbuf_tensor("identity", [P, P], F32))
        m["ident_in"] = ctx.enter_context(nc.semaphore("ident_in"))

        m["mlp_w_in"] = [ctx.enter_context(nc.semaphore(f"mlp_w_in{j}")) for j in range(2)]
        m["ring"].limit = BEFORE_MLP

        mod_stage(nc, m)
        norm_stage(nc, m, "norm_mix", m["x"], m["norm_mix_g"], scale=1, shift=0)
        scan_stage(nc, m, "hgrn")
        scan_stage(nc, m, "gla")
        pair_attention(nc, m, "diff", m["w_diff"], 4)
        merge_stage(nc, m)
        out_stage(nc, m, "out", m["x"], gate=2)
        norm_stage(nc, m, "norm_mlp", m["x1"], m["norm_mlp_g"], scale=4, shift=3,
                   ahead=mlp_ahead(m))
        mlp_stage(nc, m)
        m["ring"].limit = m["ring"].total
        norm_stage(nc, m, "norm_final", m["x1"], m["final_norm_g"], keep=m["x1"], turned=False)
        norm_stage(nc, m, "norm_even", m["x1"], m["norm_mix_2_0"])
        spatial_stage(nc, m)
        pair_attention(nc, m, "even", m["w_even"], 6)
        out_stage(nc, m, "out_even", m["x1"])
        norm_stage(nc, m, "norm_moe0", m["x1"], m["norm_ffn_2_0"], keep=m["h"])
        moe_stage(nc, m, 0)
        norm_stage(nc, m, "norm_odd", m["x1"], m["norm_mix_2_1"])
        mla_attention(nc, m)
        pair_attention(nc, m, "gqa", m["w_gqa"], 4)
        out_stage(nc, m, "out_odd", m["x1"])
        norm_stage(nc, m, "norm_moe1", m["x1"], m["norm_ffn_2_1"], keep=m["h"])
        moe_stage(nc, m, 1)
        norm_stage(nc, m, "norm_last", m["x1"], m["final_norm_2"], keep=out[0, :, :], turned=False)


def slot_of(w, k, n):
    out = np.zeros((P, SLOT), np.float32)
    out[:, :k * n] = w.reshape(k, P, n).transpose(1, 0, 2).reshape(P, k * n)
    return out


BEFORE_MLP = 12 + 2 + 8 + 2


def weight_slots(a):
    slots = []

    def dense(w):
        for c in range(0, w.shape[1], HALF):
            part = w[:, c:c + HALF]
            slots.append(slot_of(part, KD, part.shape[1]))

    dense(a["ada_w"][0])
    w_in = a["w_in"][0]
    slots.append(slot_of(np.concatenate([w_in[:, 2816:3072], w_in[:, 3584:3616]], 1), KD, 288))
    slots.append(slot_of(w_in[:, 3072:3584], KD, HALF))
    up = np.concatenate([a["w_up_a"][0], a["w_up_b"][0], a["w_up_c"][0]], 0)
    for half in range(2):
        c = half * HALF
        for branch in range(3):
            o = 3616 + branch * D + c
            slots.append(slot_of(w_in[:, o:o + HALF], KD, HALF))
        slots.append(slot_of(up[:, c:c + HALF], KD, HALF))
    dense(a["w_out"][0])

    def experts(layer):
        for e in range(17):
            if e < 16:
                slots.append(slot_of(a["moe_w_gate_2"][layer, e], KD, HALF))
                slots.append(slot_of(a["moe_w_up_2"][layer, e], KD, HALF))
            if e:
                slots.append(slot_of(a["moe_w_down_2"][layer, e - 1], 4, D))

    w = a["even_w_in_2"][0]
    dense(w[:, 2304:2816])
    dense(a["even_w_out_2"][0])
    experts(0)
    slots.append(slot_of(a["odd_w_in_2"][0][:, 0:416], KD, 416))
    dense(a["odd_w_out_2"][0])
    experts(1)
    return np.stack(slots)


def rows_on_partitions(v):
    return np.ascontiguousarray(np.broadcast_to(v.reshape(1, -1), (P, v.size)))


def k_tiles(w):
    k = w.shape[0] // P
    return w.reshape(k, P, w.shape[1]).transpose(1, 0, 2).reshape(P, -1)


def toeplitz(f):
    return f(np.arange(1920)[None, :] - 896 - np.arange(P)[:, None]).astype(np.float32)


def rope_table(pos, half, theta):
    inv = np.power(np.float32(theta), -np.arange(half, dtype=np.float32) * np.float32(2.0 / (2 * half)))
    ang = pos.astype(np.float32)[:, None] * inv[None, :].astype(np.float32)
    return np.cos(ang).astype(np.float32), np.sin(ang).astype(np.float32)


def token_tiles(t):
    return t.reshape(NT, P, -1).transpose(1, 0, 2).reshape(P, -1)


def constants():
    c = {"ident": np.eye(P, dtype=np.float32)}
    c["alibi"] = np.stack([toeplitz(lambda d: -np.abs(d) * 2.0 ** (-2 * (h + 1)) * 8.0) for h in range(4)])

    def times(d):
        a = np.abs(d)
        n = (a <= 64).astype(int) + ((a <= 256) & (a % 4 == 0)) + (a % 16 == 0)
        return np.where(n > 0, np.log(np.maximum(n, 1)) * 8.0, -1e30)
    c["dilated"] = toeplitz(times)
    idx = np.arange(P)
    masks = [idx[:, None] == idx[None, :]]
    for l in range(1, 8):
        size = 1 << l
        same = idx[:, None] // size == idx[None, :] // size
        masks.append(same & (idx[:, None] // (size // 2) != idx[None, :] // (size // 2)))
    c["levels"] = np.stack(masks, 1).astype(np.float32).reshape(P, 8 * P)
    restart = np.ones((P, S), np.float32)
    restart[:, ::P] = 0
    c["restart"] = restart
    c["own64"] = (idx[:, None] // 64 == np.arange(128)[None, :] // 64).astype(np.float32)
    c["own32"] = (idx[:, None] // 32 == np.arange(256)[None, :] // 64).astype(np.float32)
    pos = np.arange(S)
    for name, p_, half, theta in (("even", pos, 8, 500000.0), ("mla", pos, 16, 500000.0),
                                  ("row", pos // 64, 16, 10000.0), ("col", pos % 64, 16, 10000.0)):
        cos, sin = rope_table(p_, half, theta)
        c[f"cos_{name}"], c[f"sin_{name}"] = token_tiles(cos), token_tiles(sin)
    return c


def layouts(a):
    w_in, w_even, w_odd = a["w_in"][0], a["even_w_in_2"][0], a["odd_w_in_2"][0]
    d = dict(constants())
    d["w_all"] = weight_slots(a)
    d["x"] = a["x"][0]
    d["c_col"] = np.ascontiguousarray(a["c"][0].reshape(KD, P).T)
    d["ada_b"] = rows_on_partitions(a["ada_b"][0])
    d["w_diff"] = np.stack([k_tiles(np.concatenate([w_in[:, o + h * P:o + (h + 1) * P] for o in (0, 512, 1024)], 1))
                            for h in range(4)])
    w1, w2 = a["mlp_w1"][0], a["mlp_w2"][0]
    d["w_mlp"] = np.stack([s for c in range(0, 4 * D, HALF)
                           for s in (slot_of(w1[:, c:c + HALF], KD, HALF), slot_of(w2[c:c + HALF, :], 4, D))])
    d["w_hgrn"] = np.stack([k_tiles(np.concatenate([w_in[:, o + j * P:o + (j + 1) * P]
                                                    for o in (1536, 1792, 2048, 2304, 2560)], 1)) for j in range(2)])
    d["w_even"] = np.stack([k_tiles(np.concatenate([w_even[:, o + h * P:o + (h + 1) * P] for o in (0, 768, 1536)], 1))
                            for h in range(6)])
    pairs = []
    for h in range(4):
        q = w_odd[:, 416 + h * P:416 + (h + 1) * P]
        k = w_odd[:, 928 + (h // 2) * 64:928 + (h // 2 + 1) * 64]
        v = w_odd[:, 1056 + (h // 2) * 64:1056 + (h // 2 + 1) * 64]
        pairs.append(k_tiles(np.concatenate([q, k, k, v, v], 1)))
    d["w_gqa"] = np.stack(pairs)
    cq, ckv = a["odd_w_cq_up_2"][0], a["odd_w_ckv_up_2"][0]
    d["w_mla"] = np.stack([np.concatenate([k_tiles(cq[:, h * 96:(h + 1) * 96]), ckv[:, h * P:(h + 1) * P]], 1)
                           for h in range(8)])
    for name in ("norm_mix_g", "norm_mlp_g", "diff_subln_g", "hgrn_norm_g", "gla_norm_g", "final_norm_g",
                 "even_gmlp_norm_2", "odd_cq_norm_2", "odd_ckv_norm_2", "odd_dq_norm_2", "odd_dk_norm_2",
                 "final_norm_2"):
        d[name] = rows_on_partitions(a[name])
    for name in ("norm_mix_2", "norm_ffn_2"):
        for l in range(2):
            d[f"{name}_{l}"] = rows_on_partitions(a[name][l])
    d["diff_lambda"] = rows_on_partitions(a["diff_lambda"][0])
    d["lb_logits"] = np.ascontiguousarray(a["hgrn_lb_logits"][0].reshape(2, 2, P).transpose(2, 1, 0).reshape(P, 4))
    d["gate_w2"] = np.ascontiguousarray(a["gla_gate_w2"][0].transpose(1, 0, 2).reshape(16, 2 * P))
    d["gate_b"] = np.ascontiguousarray(a["gla_gate_b"][0].T)
    d["w_spatial"] = np.ascontiguousarray(a["even_w_spatial_2"][0].transpose(2, 0, 1).reshape(P, 4 * P))
    d["b_spatial"] = np.ascontiguousarray(a["even_b_spatial_2"][0].T)
    for l in range(2):
        d[f"w_router_{l}"] = k_tiles(a["moe_w_router_2"][l])
    return {k: np.ascontiguousarray(v) for k, v in d.items()}


def kernel(**inputs):
    import concourse.bacc as bacc
    from concourse.bass_utils import run_bass_kernel_spmd

    arrays = layouts({k: np.asarray(v) for k, v in inputs.items()})
    nc = bacc.Bacc("TRN2", target_bir_lowering=False, num_devices=1)
    m = {}
    for name, a in arrays.items():
        m[name] = nc.dram_tensor(f"in_{name}", a.shape, mybir.dt.from_np(a.dtype), kind="ExternalInput").ap()
    out = nc.dram_tensor("out", (1, S, D), F32, kind="ExternalOutput").ap()
    build_program(nc, m, out)
    r = run_bass_kernel_spmd(nc, [{f"in_{k}": v for k, v in arrays.items()}], core_ids=[0])
    return r.results[0]["out"]
```
